# Optimizing a Trainium2 kernel written in Bass

```python
import math
import jax, jax.numpy as jnp
from jax import lax
import numpy as np

D_MODEL = 1024
BATCH = 1
SEQ = 256
DEPTH = 2

SC_GROUPS = 8
SC_WIDTH = 512
SC_WIDTH_CONV = 3
CF_GROUPS = 8
CF_WIDTH = 512
CF_WIDTH_CONV = 31
EV_IN = 3 * SC_WIDTH + 2 * CF_WIDTH
EV_OUT_IN = SC_WIDTH + CF_WIDTH

LRU_HEADS = 8
LRU_WIDTH = 512
LRU_BLOCK = LRU_WIDTH // LRU_HEADS
LRU_CONV = 4
LRU_C = 8.0
DIL_PATTERNS = ((128, 1), (512, 4), (2048, 16))
N_DIL_GROUPS = len(DIL_PATTERNS)
DIL_HEADS = 4
DIL_HEAD_DIM = 64
DIL_OUT = DIL_HEADS * DIL_HEAD_DIM
DIL_QKV = N_DIL_GROUPS * DIL_OUT
ATTN_BLOCK = 128
OD_IN = 2 * LRU_WIDTH + 3 * DIL_QKV
OD_OUT_IN = LRU_WIDTH + DIL_OUT

D_FF = 2816
FFN_CONV = 3

N_EVEN = (DEPTH + 1) // 2
N_ODD = DEPTH // 2
EPS = 1e-6


def rmsnorm(x, g):
    xf = x.astype(jnp.float32)
    y = xf * lax.rsqrt(jnp.mean(xf * xf, axis=-1, keepdims=True) + EPS)
    return (y * g.astype(jnp.float32)).astype(x.dtype)

def layernorm(x, g, b):
    xf = x.astype(jnp.float32)
    mu = jnp.mean(xf, axis=-1, keepdims=True)
    var = jnp.mean(jnp.square(xf - mu), axis=-1, keepdims=True)
    y = (xf - mu) * lax.rsqrt(var + EPS) * g.astype(jnp.float32) + b.astype(jnp.float32)
    return y.astype(x.dtype)

def causal_dwconv(x, w):
    K, C = w.shape
    return lax.conv_general_dilated(
        x, w[:, None, :].astype(x.dtype), window_strides=(1,), padding=[(K - 1, 0)],
        dimension_numbers=("NWC", "WIO", "NWC"), feature_group_count=C)

def even_mixer(h, w_in, sc_conv_w, cf_conv_w, cf_conv_b, cf_ln_g, cf_ln_b, w_out):
    z = h @ w_in
    sc_b, sc_c, sc_x, cf_a, cf_g = jnp.split(
        z, [SC_WIDTH, 2 * SC_WIDTH, 3 * SC_WIDTH, 3 * SC_WIDTH + CF_WIDTH], axis=-1)
    y_sc = sc_b * causal_dwconv(sc_c * sc_x, sc_conv_w)
    u = cf_a * jax.nn.sigmoid(cf_g)
    u = causal_dwconv(u, cf_conv_w) + cf_conv_b
    u = jax.nn.silu(layernorm(u, cf_ln_g, cf_ln_b))
    return jnp.concatenate([y_sc, u], axis=-1) @ w_out

def rg_lru(xc, w_a, b_a, w_x, b_x, lam):
    B, S, W = xc.shape
    xb = xc.reshape(B, S, LRU_HEADS, LRU_BLOCK)
    r = jax.nn.sigmoid(jnp.einsum("bshi,hij->bshj", xb, w_a).reshape(B, S, W) + b_a)
    i = jax.nn.sigmoid(jnp.einsum("bshi,hij->bshj", xb, w_x).reshape(B, S, W) + b_x)
    log_a = -LRU_C * r.astype(jnp.float32) * jax.nn.softplus(-lam.astype(jnp.float32))
    a = jnp.exp(log_a)
    mult = jnp.sqrt(-jnp.expm1(2.0 * log_a))
    bt = mult * (i * xc).astype(jnp.float32)

    def combine(left, right):
        a1, b1 = left
        a2, b2 = right
        return a1 * a2, a2 * b1 + b2

    _, hs = lax.associative_scan(combine, (a, bt), axis=1)
    return hs.astype(xc.dtype)

def dilated_group_attention(q, k, v, window, dilation):
    B, S, H, Dh = q.shape
    L = S // dilation
    nb = -(-L // ATTN_BLOCK)
    Lp = nb * ATTN_BLOCK
    span = window // dilation

    def strided(t):
        t = t.reshape(B, L, dilation, H, Dh).transpose(0, 2, 1, 3, 4)
        t = jnp.pad(t, ((0, 0), (0, 0), (0, Lp - L), (0, 0), (0, 0)))
        return t.reshape(B, dilation, nb, ATTN_BLOCK, H, Dh)

    def with_prev(t):
        prev = jnp.pad(t[:, :, :-1], ((0, 0), (0, 0), (1, 0), (0, 0), (0, 0), (0, 0)))
        return jnp.concatenate([prev, t], axis=3)

    qb = strided(q)
    kk = with_prev(strided(k))
    vv = with_prev(strided(v))
    s = jnp.einsum("brnqhd,brnkhd->brnhqk", qb, kk).astype(jnp.float32)
    qi = jnp.arange(ATTN_BLOCK)[:, None]
    kj = jnp.arange(2 * ATTN_BLOCK)[None, :]
    steps = ATTN_BLOCK + qi - kj
    band = (steps >= 0) & (steps <= span)
    blk_idx = jnp.arange(nb)[:, None, None]
    mask = band[None] & ((blk_idx > 0) | (kj >= ATTN_BLOCK)[None])
    s = jnp.where(mask[None, None, :, None], s, -jnp.inf)
    m = jnp.max(s, axis=-1, keepdims=True)
    p = jnp.exp(s - m)
    den = jnp.sum(p, axis=-1, keepdims=True)
    o = jnp.einsum("brnhqk,brnkhd->brnqhd", p, vv.astype(jnp.float32))
    o = o / jnp.swapaxes(den, 3, 4)
    lse = jnp.swapaxes((m + jnp.log(den))[..., 0], 3, 4)
    o = o.reshape(B, dilation, Lp, H, Dh)[:, :, :L].transpose(0, 2, 1, 3, 4).reshape(B, S, H, Dh)
    lse = lse.reshape(B, dilation, Lp, H)[:, :, :L].transpose(0, 2, 1, 3).reshape(B, S, H)
    return o, lse

def dilated_attention(q, k, v, q_norm_g, k_norm_g):
    B, S, _ = q.shape
    shp = (B, S, N_DIL_GROUPS, DIL_HEADS, DIL_HEAD_DIM)
    qn = rmsnorm(q.reshape(shp), q_norm_g) * (DIL_HEAD_DIM ** -0.5)
    kn = rmsnorm(k.reshape(shp), k_norm_g)
    vr = v.reshape(shp)
    outs, lses = [], []
    for g, (window, dilation) in enumerate(DIL_PATTERNS):
        o, lse = dilated_group_attention(qn[:, :, g], kn[:, :, g], vr[:, :, g], window, dilation)
        outs.append(o)
        lses.append(lse)
    o = jnp.stack(outs)
    wts = jax.nn.softmax(jnp.stack(lses), axis=0)
    out = jnp.einsum("gbsh,gbshd->bshd", wts, o)
    return out.reshape(B, S, DIL_OUT).astype(q.dtype)

def odd_mixer(h, w_in, lru_conv_w, lru_conv_b, lru_wa, lru_ba, lru_wx, lru_bx, lru_lam,
              q_norm_g, k_norm_g, w_out):
    z = h @ w_in
    lru_x, lru_gate, q, k, v = jnp.split(
        z, [LRU_WIDTH, 2 * LRU_WIDTH, 2 * LRU_WIDTH + DIL_QKV, 2 * LRU_WIDTH + 2 * DIL_QKV], axis=-1)
    xc = causal_dwconv(lru_x, lru_conv_w) + lru_conv_b
    y_lru = rg_lru(xc, lru_wa, lru_ba, lru_wx, lru_bx, lru_lam) * jax.nn.gelu(lru_gate)
    y_att = dilated_attention(q, k, v, q_norm_g, k_norm_g)
    return jnp.concatenate([y_lru, y_att], axis=-1) @ w_out

def conv_glu_ffn(h, w_gate, w_up, conv_w, conv_b, w_down):
    g = causal_dwconv(h @ w_gate, conv_w) + conv_b
    return (jax.nn.silu(g) * (h @ w_up)) @ w_down

def first_inputs(seed: int = 0) -> dict:
    key = jax.random.key(seed)
    ks = iter(jax.random.split(key, 40))
    f32 = jnp.float32

    def nrm(shape, fan_in):
        return jax.random.normal(next(ks), shape, f32) * (fan_in ** -0.5)

    def gain(shape):
        return 1.0 + 0.05 * jax.random.normal(next(ks), shape, f32)

    def bias(shape):
        return 0.01 * jax.random.normal(next(ks), shape, f32)

    u = jax.random.uniform(next(ks), (N_ODD, LRU_WIDTH), f32, minval=0.9, maxval=0.999)
    a0 = u ** (1.0 / LRU_C)
    lam = jnp.log(a0) - jnp.log1p(-a0)

    return {
        "x": jax.random.normal(next(ks), (BATCH, SEQ, D_MODEL), f32),
        "mix_norm_g": gain((DEPTH, D_MODEL)),
        "ffn_norm_g": gain((DEPTH, D_MODEL)),
        "ev_w_in": nrm((N_EVEN, D_MODEL, EV_IN), D_MODEL),
        "ev_sc_conv_w": nrm((N_EVEN, SC_WIDTH_CONV, SC_WIDTH), SC_WIDTH_CONV),
        "ev_cf_conv_w": nrm((N_EVEN, CF_WIDTH_CONV, CF_WIDTH), CF_WIDTH_CONV),
        "ev_cf_conv_b": bias((N_EVEN, CF_WIDTH)),
        "ev_cf_ln_g": gain((N_EVEN, CF_WIDTH)),
        "ev_cf_ln_b": bias((N_EVEN, CF_WIDTH)),
        "ev_w_out": nrm((N_EVEN, EV_OUT_IN, D_MODEL), EV_OUT_IN),
        "od_w_in": nrm((N_ODD, D_MODEL, OD_IN), D_MODEL),
        "od_lru_conv_w": nrm((N_ODD, LRU_CONV, LRU_WIDTH), LRU_CONV),
        "od_lru_conv_b": bias((N_ODD, LRU_WIDTH)),
        "od_lru_wa": nrm((N_ODD, LRU_HEADS, LRU_BLOCK, LRU_BLOCK), LRU_BLOCK),
        "od_lru_ba": bias((N_ODD, LRU_WIDTH)),
        "od_lru_wx": nrm((N_ODD, LRU_HEADS, LRU_BLOCK, LRU_BLOCK), LRU_BLOCK),
        "od_lru_bx": bias((N_ODD, LRU_WIDTH)),
        "od_lru_lam": lam,
        "od_q_norm_g": gain((N_ODD, DIL_HEAD_DIM)),
        "od_k_norm_g": gain((N_ODD, DIL_HEAD_DIM)),
        "od_w_out": nrm((N_ODD, OD_OUT_IN, D_MODEL), OD_OUT_IN),
        "ffn_w_gate": nrm((DEPTH, D_MODEL, D_FF), D_MODEL),
        "ffn_w_up": nrm((DEPTH, D_MODEL, D_FF), D_MODEL),
        "ffn_conv_w": nrm((DEPTH, FFN_CONV, D_FF), FFN_CONV),
        "ffn_conv_b": bias((DEPTH, D_FF)),
        "ffn_w_down": nrm((DEPTH, D_FF, D_MODEL), D_FF),
    }

def first_block(x, mix_norm_g, ffn_norm_g,
              ev_w_in, ev_sc_conv_w, ev_cf_conv_w, ev_cf_conv_b, ev_cf_ln_g, ev_cf_ln_b, ev_w_out,
              od_w_in, od_lru_conv_w, od_lru_conv_b, od_lru_wa, od_lru_ba, od_lru_wx, od_lru_bx,
              od_lru_lam, od_q_norm_g, od_k_norm_g, od_w_out,
              ffn_w_gate, ffn_w_up, ffn_conv_w, ffn_conv_b, ffn_w_down):
    for layer in range(DEPTH):
        j = layer // 2
        h = rmsnorm(x, mix_norm_g[layer])
        if layer % 2 == 0:
            x = x + even_mixer(h, ev_w_in[j], ev_sc_conv_w[j], ev_cf_conv_w[j], ev_cf_conv_b[j],
                               ev_cf_ln_g[j], ev_cf_ln_b[j], ev_w_out[j])
        else:
            x = x + odd_mixer(h, od_w_in[j], od_lru_conv_w[j], od_lru_conv_b[j], od_lru_wa[j],
                              od_lru_ba[j], od_lru_wx[j], od_lru_bx[j], od_lru_lam[j],
                              od_q_norm_g[j], od_k_norm_g[j], od_w_out[j])
        h = rmsnorm(x, ffn_norm_g[layer])
        x = x + conv_glu_ffn(h, ffn_w_gate[layer], ffn_w_up[layer], ffn_conv_w[layer],
                             ffn_conv_b[layer], ffn_w_down[layer])
    return x


MIX_WIDTH = D_MODEL
POOL_WIDTH = MIX_WIDTH // 2
POOL_WINDOWS = (2, 4, 8, 16)
POOL_GROUPS = len(POOL_WINDOWS)
POOL_GC = POOL_WIDTH // POOL_GROUPS
N_HEADS = 4
QK_NOPE = 128
QK_ROPE = 64
V_HEAD = 128
QK_HEAD = QK_NOPE + QK_ROPE
MLA_WIDTH = N_HEADS * V_HEAD
Q_LORA = 384
KV_LORA = 256
ROPE_THETA = 10000.0
SOFTMAX_SCALE = 1.0 / math.sqrt(QK_HEAD)
Q_BLOCK = 128
IN_COLS = POOL_WIDTH + Q_LORA + KV_LORA + QK_ROPE
N_SUBLAYERS = 3


def rms_norm(x, g):
    xf = x.astype(jnp.float32)
    y = xf * lax.rsqrt(jnp.mean(xf * xf, axis=-1, keepdims=True) + EPS)
    return (y * g.astype(jnp.float32)).astype(x.dtype)

def modulate(h, shift, scale):
    return h * (1 + scale[:, None, :]) + shift[:, None, :]

def swiglu(h, w_gate, w_up, w_down):
    return (jax.nn.silu(h @ w_gate) * (h @ w_up)) @ w_down

def rotate_half(x):
    x1, x2 = jnp.split(x, 2, axis=-1)
    return jnp.concatenate([-x2, x1], axis=-1)

def apply_rope(x, cos, sin):
    return x * cos + rotate_half(x) * sin

def causal_multiscale_pool(u, pool_w, pool_scale):
    B, S, C = u.shape
    cs = jnp.cumsum(u.astype(jnp.float32), axis=1)
    pos = jnp.arange(S)
    means = []
    for g, w in enumerate(POOL_WINDOWS):
        csg = cs[..., g * POOL_GC:(g + 1) * POOL_GC]
        lag = jnp.pad(csg, ((0, 0), (w, 0), (0, 0)))[:, :S]
        cnt = jnp.minimum(pos + 1, w).astype(jnp.float32)[None, :, None]
        means.append((csg - lag) / cnt)
    pooled = jnp.stack(means, axis=2).astype(u.dtype)
    diff = pooled - u.reshape(B, S, POOL_GROUPS, POOL_GC)
    y = jnp.einsum('bsgc,gcd->bsgd', diff, pool_w).reshape(B, S, C)
    return y * pool_scale

def mla_attention(cq, ckv, kr, q_a_norm, w_q_b, kv_a_norm, w_kv_b, cos, sin):
    B, S, _ = cq.shape
    q = (rms_norm(cq, q_a_norm) @ w_q_b).reshape(B, S, N_HEADS, QK_HEAD)
    q_nope, q_rope = q[..., :QK_NOPE], q[..., QK_NOPE:]
    q_rope = apply_rope(q_rope, cos[:, :, None, :], sin[:, :, None, :])
    kv = (rms_norm(ckv, kv_a_norm) @ w_kv_b).reshape(B, S, N_HEADS, QK_NOPE + V_HEAD)
    k_nope, v = kv[..., :QK_NOPE], kv[..., QK_NOPE:]
    k_rope = apply_rope(kr, cos, sin)

    nb = S // Q_BLOCK
    qn = q_nope.reshape(B, nb, Q_BLOCK, N_HEADS, QK_NOPE).transpose(1, 0, 3, 2, 4)
    qr = q_rope.reshape(B, nb, Q_BLOCK, N_HEADS, QK_ROPE).transpose(1, 0, 3, 2, 4)
    kn = k_nope.transpose(0, 2, 1, 3)
    vv = v.transpose(0, 2, 1, 3)
    kpos = jnp.arange(S)

    def block(args):
        qn_b, qr_b, i = args
        s = (jnp.einsum('bhqd,bhkd->bhqk', qn_b, kn)
             + jnp.einsum('bhqd,bkd->bhqk', qr_b, k_rope)).astype(jnp.float32) * SOFTMAX_SCALE
        qpos = i * Q_BLOCK + jnp.arange(Q_BLOCK)
        s = jnp.where(qpos[:, None] >= kpos[None, :], s, -jnp.inf)
        p = jax.nn.softmax(s, axis=-1).astype(vv.dtype)
        return jnp.einsum('bhqk,bhkd->bhqd', p, vv)

    o = lax.map(block, (qn, qr, jnp.arange(nb)))
    return o.transpose(1, 0, 3, 2, 4).reshape(B, S, MLA_WIDTH)

def second_inputs(seed: int = 0) -> dict:
    key = jax.random.key(seed)
    ks = jax.random.split(key, 24)
    f32 = jnp.float32
    nrm = lambda k, shape, s: (jax.random.normal(k, shape, f32) * s)
    gain = lambda k, shape: 1.0 + 0.05 * jax.random.normal(k, shape, f32)
    D, F, L = D_MODEL, D_FF, DEPTH
    x = jax.random.normal(ks[0], (BATCH, SEQ, D), f32)
    c = jax.random.normal(ks[1], (BATCH, D), f32)
    positions = jnp.broadcast_to(jnp.arange(SEQ, dtype=jnp.int32)[None, :], (BATCH, SEQ))
    return {
        "x": x,
        "c": c,
        "positions": positions,
        "ada_w": nrm(ks[2], (L, D, 3 * N_SUBLAYERS * D), 0.5 * D ** -0.5),
        "ada_b": nrm(ks[3], (L, 3 * N_SUBLAYERS * D), 0.01),
        "ffn1_norm": gain(ks[4], (L, D)),
        "ffn1_w_gate": nrm(ks[5], (L, D, F), D ** -0.5),
        "ffn1_w_up": nrm(ks[6], (L, D, F), D ** -0.5),
        "ffn1_w_down": nrm(ks[7], (L, F, D), F ** -0.5),
        "mix_norm": gain(ks[8], (L, D)),
        "w_in": nrm(ks[9], (L, D, IN_COLS), D ** -0.5),
        "pool_w": nrm(ks[10], (L, POOL_GROUPS, POOL_GC, POOL_GC), POOL_GC ** -0.5),
        "pool_scale": gain(ks[11], (L, POOL_WIDTH)),
        "q_a_norm": gain(ks[12], (L, Q_LORA)),
        "w_q_b": nrm(ks[13], (L, Q_LORA, N_HEADS * QK_HEAD), Q_LORA ** -0.5),
        "kv_a_norm": gain(ks[14], (L, KV_LORA)),
        "w_kv_b": nrm(ks[15], (L, KV_LORA, N_HEADS * (QK_NOPE + V_HEAD)), KV_LORA ** -0.5),
        "w_out": nrm(ks[16], (L, MIX_WIDTH, D), MIX_WIDTH ** -0.5),
        "ffn2_norm": gain(ks[17], (L, D)),
        "ffn2_w_gate": nrm(ks[18], (L, D, F), D ** -0.5),
        "ffn2_w_up": nrm(ks[19], (L, D, F), D ** -0.5),
        "ffn2_w_down": nrm(ks[20], (L, F, D), F ** -0.5),
        "final_norm": gain(ks[21], (D,)),
    }

def second_block(x, c, positions, ada_w, ada_b, ffn1_norm, ffn1_w_gate, ffn1_w_up, ffn1_w_down,
              mix_norm, w_in, pool_w, pool_scale, q_a_norm, w_q_b, kv_a_norm, w_kv_b, w_out,
              ffn2_norm, ffn2_w_gate, ffn2_w_up, ffn2_w_down, final_norm):
    inv_freq = 1.0 / (ROPE_THETA ** (jnp.arange(0, QK_ROPE, 2, dtype=jnp.float32) / QK_ROPE))
    ang = positions.astype(jnp.float32)[..., None] * inv_freq
    ang = jnp.concatenate([ang, ang], axis=-1)
    cos = jnp.cos(ang).astype(x.dtype)
    sin = jnp.sin(ang).astype(x.dtype)
    c_act = jax.nn.silu(c)

    for l in range(DEPTH):
        mod = c_act @ ada_w[l] + ada_b[l]
        (sh1, sc1, g1, sh2, sc2, g2, sh3, sc3, g3) = jnp.split(mod, 3 * N_SUBLAYERS, axis=-1)

        h = modulate(rms_norm(x, ffn1_norm[l]), sh1, sc1)
        x = x + 0.5 * g1[:, None, :] * swiglu(h, ffn1_w_gate[l], ffn1_w_up[l], ffn1_w_down[l])

        h = modulate(rms_norm(x, mix_norm[l]), sh2, sc2)
        z = h @ w_in[l]
        o1 = POOL_WIDTH
        o2 = o1 + Q_LORA
        o3 = o2 + KV_LORA
        y_pool = causal_multiscale_pool(z[..., :o1], pool_w[l], pool_scale[l])
        y_mla = mla_attention(z[..., o1:o2], z[..., o2:o3], z[..., o3:], q_a_norm[l], w_q_b[l],
                              kv_a_norm[l], w_kv_b[l], cos, sin)
        y = jnp.concatenate([y_pool, y_mla], axis=-1) @ w_out[l]
        x = x + g2[:, None, :] * y

        h = modulate(rms_norm(x, ffn2_norm[l]), sh3, sc3)
        x = x + 0.5 * g3[:, None, :] * swiglu(h, ffn2_w_gate[l], ffn2_w_up[l], ffn2_w_down[l])

    return rms_norm(x, final_norm)


def setup_inputs(seed=0):
    out = dict(first_inputs(seed))
    for name, value in second_inputs(seed + 1).items():
        if name != "x":
            out[name + "_2"] = value
    return out


def reference(
    x, mix_norm_g, ffn_norm_g, ev_w_in, ev_sc_conv_w, ev_cf_conv_w, ev_cf_conv_b, ev_cf_ln_g,
    ev_cf_ln_b, ev_w_out, od_w_in, od_lru_conv_w, od_lru_conv_b, od_lru_wa, od_lru_ba,
    od_lru_wx, od_lru_bx, od_lru_lam, od_q_norm_g, od_k_norm_g, od_w_out, ffn_w_gate, ffn_w_up,
    ffn_conv_w, ffn_conv_b, ffn_w_down, c_2, positions_2, ada_w_2, ada_b_2, ffn1_norm_2,
    ffn1_w_gate_2, ffn1_w_up_2, ffn1_w_down_2, mix_norm_2, w_in_2, pool_w_2, pool_scale_2,
    q_a_norm_2, w_q_b_2, kv_a_norm_2, w_kv_b_2, w_out_2, ffn2_norm_2, ffn2_w_gate_2,
    ffn2_w_up_2, ffn2_w_down_2, final_norm_2,
):
    x = first_block(
        x, mix_norm_g, ffn_norm_g, ev_w_in, ev_sc_conv_w, ev_cf_conv_w, ev_cf_conv_b,
        ev_cf_ln_g, ev_cf_ln_b, ev_w_out, od_w_in, od_lru_conv_w, od_lru_conv_b, od_lru_wa,
        od_lru_ba, od_lru_wx, od_lru_bx, od_lru_lam, od_q_norm_g, od_k_norm_g, od_w_out,
        ffn_w_gate, ffn_w_up, ffn_conv_w, ffn_conv_b, ffn_w_down,
    )
    return second_block(
        x, c_2, positions_2, ada_w_2, ada_b_2, ffn1_norm_2, ffn1_w_gate_2, ffn1_w_up_2,
        ffn1_w_down_2, mix_norm_2, w_in_2, pool_w_2, pool_scale_2, q_a_norm_2, w_q_b_2,
        kv_a_norm_2, w_kv_b_2, w_out_2, ffn2_norm_2, ffn2_w_gate_2, ffn2_w_up_2, ffn2_w_down_2,
        final_norm_2,
    )


_drawn_inputs = setup_inputs


def setup_inputs(seed=0):
    import zlib

    import numpy as np

    out = dict(_drawn_inputs(seed))
    spreads = {}
    factors = {'ev_cf_conv_b': 4.728,
     'ev_cf_ln_b': 8.0,
     'od_lru_conv_b': 3.863,
     'od_lru_ba': 32.679,
     'od_lru_bx': 8.0,
     'od_q_norm_g': 8.0,
     'od_k_norm_g': 8.0,
     'ffn_conv_b': 8.0,
     'ada_b_2': 6.86,
     'ffn1_norm_2': 8.0,
     'mix_norm_2': 6.043,
     'pool_scale_2': 6.293,
     'q_a_norm_2': 8.0,
     'kv_a_norm_2': 8.0,
     'ffn2_norm_2': 8.0}
    for name, (base, spread) in spreads.items():
        noise = np.random.default_rng([zlib.crc32(name.encode()), seed]).standard_normal(out[name].shape)
        drawn = base * np.exp(spread * noise) if base else spread * noise
        out[name] = __import__('jax').numpy.asarray(drawn.astype(out[name].dtype))
    for name, factor in factors.items():
        out[name] = (out[name] * factor).astype(out[name].dtype)
    return out
```

```python
from contextlib import ExitStack

import concourse.bass as bass
from concourse import mybir

F32 = mybir.dt.float32
F32R = mybir.dt.float32r
BF16 = mybir.dt.bfloat16
I32 = mybir.dt.int32
ALU = mybir.AluOpType
ACT = mybir.ActivationFunctionType
AX = mybir.AxisListType

P = 128
D = 1024
S = 256
KD = D // P
F = 2816
FB = 256
NFB = F // FB
EPS = 1e-6
NB = S // P

RAW = 3
SPL = 3
UNIT = 2048
ADA_RING = 4
ACR = 3
N_ADA = 18

SC = CF = 512
TAPS = 31
LRU = 512
QKV = 768
QH, HN, HR, HV = 4, 128, 64, 128


def param_rows():
    r = []
    for l in range(2):
        r.append((f"mixn{l}", "mix_norm_g", (l,), 8))
        r.append((f"ffnn{l}", "ffn_norm_g", (l,), 8))
    r.append(("scw", "ev_sc_conv_w", (0,), 12))
    r.append(("cfb", "ev_cf_conv_b", (0,), 4))
    r.append(("lng", "ev_cf_ln_g", (0,), 4))
    r.append(("lnb", "ev_cf_ln_b", (0,), 4))
    r.append(("lcw", "od_lru_conv_w", (0,), 16))
    r.append(("lcb", "od_lru_conv_b", (0,), 4))
    r.append(("lba", "od_lru_ba", (0,), 4))
    r.append(("lbx", "od_lru_bx", (0,), 4))
    r.append(("lam", "od_lru_lam", (0,), 4))
    r.append(("c", "c_2", (), 8))
    r.append(("qng", "od_q_norm_g", (0,), 1))
    r.append(("kng", "od_k_norm_g", (0,), 1))
    r.append(("cfw", "ev_cf_conv_w", (0,), 124))
    for l in range(2):
        r.append((f"fcw{l}", "ffn_conv_w", (l,), 66))
        r.append((f"fcb{l}", "ffn_conv_b", (l,), 22))
    for l in range(2):
        r.append((f"adab{l}", "ada_b_2", (l,), 72))
    for l in range(2):
        r.append((f"n1{l}", "ffn1_norm_2", (l,), 8))
        r.append((f"n2{l}", "mix_norm_2", (l,), 8))
        r.append((f"n3{l}", "ffn2_norm_2", (l,), 8))
        r.append((f"ps{l}", "pool_scale_2", (l,), 4))
        r.append((f"qa{l}", "q_a_norm_2", (l,), 3))
        r.append((f"kva{l}", "kv_a_norm_2", (l,), 2))
    r.append(("fin", "final_norm_2", (), 8))
    return r


def place_params():
    cols, groups, used = {}, [[]], 0
    order = sorted(param_rows(), key=lambda e: -e[3])
    free = []
    for e in order:
        for g in range(len(free)):
            if free[g] >= e[3]:
                break
        else:
            free.append(P)
            g = len(free) - 1
        cols[e[0]] = g * P + P - free[g]
        free[g] -= e[3]
    return cols, len(free), [P - f for f in free]


PCOL, NPG, PG_ROWS = place_params()


CONST = {}


def const_layout():
    at = 0
    for name, n in (("ident", P), ("mask", 3 * 2 * P), ("ones", P), ("headones", P), ("rot", P), ("cmask", 2 * P),
                    ("krdup", P), ("krrot", P), ("edge", 4 * 16), ("freq", 1), ("eps", 1), ("one", 1)):
        CONST[name] = (at, n)
        at += n
    return at


NCONST = const_layout()


def constants():
    import numpy as np
    c = np.zeros((P, NCONST), np.float32)

    def put(name, v):
        a, n = CONST[name]
        c[:v.shape[0], a:a + n] = v.reshape(v.shape[0], n)

    put("ident", np.eye(P, dtype=np.float32))
    q = np.arange(P)[:, None]
    k = np.arange(2 * P)[None, :]
    steps = P + q - k
    m = np.zeros((P, 3, 2 * P), np.float32)
    for g, (window, dil) in enumerate(((128, 1), (512, 4), (2048, 16))):
        ok = (steps >= 0) & (steps <= window) & (steps % dil == 0)
        m[:, g] = np.where(ok, 0.0, -1e30)
    put("mask", m)
    put("cmask", np.where(steps >= 0, 0.0, -1e30).astype(np.float32))
    put("ones", np.ones((P, P), np.float32))
    h = np.zeros((P, P), np.float32)
    h[:64, :64] = h[64:, 64:] = 1.0 / 64
    put("headones", h)
    r = np.zeros((64, 64), np.float32)
    for i in range(32):
        r[i + 32, i] = -1.0
        r[i, i + 32] = 1.0
    rr = np.zeros((P, P), np.float32)
    rr[:64, :64] = rr[64:, 64:] = r
    put("rot", rr)
    put("krdup", np.concatenate([np.eye(64), np.eye(64)], 1).astype(np.float32))
    put("krrot", np.concatenate([r, r], 1))
    e = np.zeros((P, 4, 16), np.float32)
    for g in range(4):
        w = 2 ** (g + 1)
        e[:, g] = (w / np.minimum(np.arange(16) + 1, w)).astype(np.float32)
    put("edge", e)
    inv = (np.float32(1.0) / np.power(np.float32(10000.0), np.arange(0, 64, 2, dtype=np.float32) / np.float32(64))).astype(np.float32)
    put("freq", np.tile(inv, 4)[:, None])
    put("eps", np.full((P, 1), EPS, np.float32))
    put("one", np.ones((P, 1), np.float32))
    return c


class Steps:

    def __init__(self, eng, sem):
        self.eng, self.sem, self.n = eng, sem, 0

    def mark(self, ins):
        ins.then_inc(self.sem, 1)
        self.n += 1
        return self.n

    def wait(self, n):
        self.eng.wait_ge(self.sem, n)

    def link(self, ins):
        self.wait(self.mark(ins))


def stream():
    base, n = {}, 0
    for name, k in ([("ev_in", 10), ("ev_out", 4), ("ffn0", 33), ("od_in", 13), ("od_out", 4), ("ffn1", 33)]
                    + [(f"{s}{l}", k) for l in range(2) for s, k in
                       (("fa", 33), ("w_in", 5), ("q_b", 2), ("kv_b", 1), ("w_out", 4), ("fb", 33))]):
        base[name] = n
        n += k
    return base, n


U0, NUNITS = stream()
FFNS = ["ffn0", "ffn1", "fa0", "fb0", "fa1", "fb1"]
UNIT_SIZE = {}
for _l in range(2):
    UNIT_SIZE[U0[f"w_in{_l}"] + 2] = KD * 192
    UNIT_SIZE[U0[f"q_b{_l}"]] = UNIT_SIZE[U0[f"q_b{_l}"] + 1] = 3 * 384
for _i in range(4):
    UNIT_SIZE[U0["od_out"] + _i] = 6 * 256

EV_ORDER = [6, 7, 8, 9, 0, 1, 2, 3, 4, 5]
OD_ORDER = list(range(13))
W_ORDER = [2, 3, 4, 0, 1]

FILL, _n = {}, 0
for _name, _k in ([("mix0", 4), ("y_ev", 4), ("ffn0", 4), ("mix1", 4), ("y_od", 3), ("ffn1", 4)]
                  + [(f"{_s}{_l}", _k) for _l in range(2) for _s, _k in
                     (("fa", 4), ("w", 4), ("cqn", 1), ("yw", 4), ("fb", 4))]):
    FILL[_name] = _n
    _n += _k
NORMS = ["mix0", "ffn0", "mix1", "ffn1", "fa0", "w0", "fb0", "fa1", "w1", "fb1", "final"]

ADA_GAP = {"conv": 3, "ffn0": 1, "mix1": 3, "att": 2, "ffn1": 2, "fa0": 3, "w0": 3, "fb0": 1}
ADA, _a = {}, 0
for _name, _k in ADA_GAP.items():
    ADA[_name] = _a
    _a += _k
ADA["fa1"] = _a
assert _a == N_ADA

N_PAR = len(param_rows()) + 2
TWO_PI = 6.283185307179586


def two_pi_parts():
    import math
    parts, rest = [], TWO_PI
    for _ in range(3):
        e = math.floor(math.log2(rest)) - 7
        part = math.floor(rest / 2.0 ** e) * 2.0 ** e
        parts.append(part)
        rest -= part
    return parts + [rest]


def build(nc, A, const, out):
    ctx = ExitStack()
    with ctx:
        def sb(name, shape, dt=F32):
            return ctx.enter_context(nc.sbuf_tensor(name, shape, dt))

        def sem(name):
            return ctx.enter_context(nc.semaphore(name))

        raw = sb("raw", [P, RAW, UNIT])
        wh = sb("wh", [P, SPL, UNIT], F32R)
        wl = sb("wl", [P, SPL, UNIT], F32R)
        ada = sb("ada", [P, ADA_RING, D])
        AC = sb("AC", [P, ACR, D])
        X = sb("X", [P, KD, S])
        HH = sb("HH", [P, KD, S], F32R)
        HL = sb("HL", [P, KD, S], F32R)
        T = sb("T", [P, KD, S])
        Z = sb("Z", [P, 6672])
        WK = sb("WK", [P, 4608])
        FH = sb("FH", [P, 2, 2, S], F32R)
        FL = sb("FL", [P, 2, 2, S], F32R)
        PR = sb("PR", [P, NPG * P])
        MOD = sb("MOD", [P, N_ADA * KD])
        CN = sb("CN", [P, NCONST])
        GM = sb("GM", [P, 6, KD])
        HG = sb("HG", [P, 4, KD])
        CA = sb("CA", [P, KD])
        SM = sb("SM", [P, 48])
        COS = sb("COS", [P, S])
        SIN = sb("SIN", [P, S])
        RT = sb("RT", [P, 512])
        RS = sb("RS", [P, 512])
        ZB = sb("ZB", [P, P], BF16)
        PW = sb("PW", [P, 4, P])
        PX = WK[:, 4096:4608].rearrange("p (t c) -> p t c", c=P)
        PS = ctx.enter_context(nc.psum_tensor("PS", [P, 8, 512], F32))

        def bank(i, a=0, n=512, rows=slice(0, P)):
            return PS[rows, i, a:a + n]

        def banks(i, n):
            return PS[:, i:i + n, :].rearrange("p b c -> p (b c)")

        def cn(name, rows=P):
            a, n = CONST[name]
            return CN[0:rows, a:a + n]

        def pc(name, i=0, n=1):
            return PR[:, PCOL[name] + i:PCOL[name] + i + n]

        def cols(t, a, n, w=S):
            return t[:, a:a + n * w].rearrange("p (t s) -> p t s", s=w)

        def pairs(ap, w=S):
            return ap.rearrange("p (t s) -> p t s", s=w)

        def over(ap, n):
            return ap.unsqueeze(1).to_broadcast([ap.shape[0], n, ap.shape[1]])

        mask = cn("mask").rearrange("p (g k) -> p g k", g=3)

        x_in, const_in, par_in, pos_in = sem("x_in"), sem("const_in"), sem("par_in"), sem("pos_in")
        raw_in = [sem(f"raw_in{i}") for i in range(RAW)]
        hi_done = sem("hi_done")
        split_done = sem("split_done")
        w_used = sem("w_used")
        ada_in = [sem(f"ada_in{i}") for i in range(ADA_RING)]
        ada_sum = sem("ada_sum")
        ada_mul = sem("ada_mul")
        ada_used = sem("ada_used")
        ada_out = sem("ada_out")
        aux_in = [sem(f"aux_in{i}") for i in range(3)]
        dv, av = sem("dv"), sem("av")
        x_ready = sem("x_ready")
        sq_ready = sem("sq_ready")
        stat, root = sem("stat"), sem("root")
        t_ready = sem("t_ready")
        hh_ready, h_ready = sem("hh_ready"), sem("h_ready")
        acc = sem("acc")
        g_first = sem("g_first")
        g_tap = sem("g_tap")
        g_act = sem("g_act")
        f_ready = sem("f_ready")
        fh_ready, fl_ready = sem("fh_ready"), sem("fl_ready")
        z_out = sem("z_out")
        o_done = sem("o_done")
        events = {}

        def ev(name):
            if name not in events:
                events[name] = sem("ev_" + name)
            return events[name]

        EV = {"U": 0, "V": 1144, "A": 2168, "B": 3192, "C": 4216, "P": 5240}
        OD = {"Q": 0, "K": 1536, "V": 3072, "X": 4608, "G": 5644}
        ML = {"C": 0, "KX": 1280, "QN": 1536, "QR": 2560, "KN": 3072, "KR": 4096, "V": 4352, "U": 5376}

        def dilated_rounds():
            out = []
            for r, (b, heads) in enumerate(((0, (0, 1, 2, 3)), (1, (0, 1)), (1, (2, 3)))):
                nk = b + 1
                w = 3 * nk * P
                sc, va = [], []
                for i, h in enumerate(heads):
                    half = slice(64 * (h % 2), 64 * (h % 2) + 64)
                    chain = []
                    for g in range(3):
                        c = (2 * g + h // 2) * S
                        q = Z[half, OD["Q"] + c + b * P:OD["Q"] + c + (b + 1) * P]
                        k = Z[half, OD["K"] + c:OD["K"] + c + nk * P]
                        sc.append((i * w + g * nk * P, [(q, k)]))
                        for kb in range(nk):
                            v = Z[:, OD["V"] + kb * QKV + (4 * g + h) * 64:][:, 0:64]
                            chain.append((v, (i * w) // P + g * nk + kb))
                    va.append((PS[half, 7, (h // 2) * P:(h // 2 + 1) * P], chain))
                sc.sort(key=lambda e: (e[0] // w) % 2)
                m = mask[:, :, P:2 * P] if b == 0 else mask
                out.append({"b": b, "heads": heads, "w": w, "s": 0, "ns": 3, "pt": 3, "o": 7, "scores": sc,
                            "values": va, "S": (r % 2) * 1536, "PT": 3072, "scale": 1.0,
                            "masks": [(0, 3 * nk * P, m)]})
            return out

        def latent_rounds():
            out = []
            for b in range(NB):
                nk = b + 1
                w = nk * P
                sc, va = [], []
                for h in range(QH):
                    half = slice(64 * (h % 2), 64 * (h % 2) + 64)
                    sc.append((h * w, [
                        (Z[:, ML["QN"] + h * S + b * P:][:, 0:P], Z[:, ML["KN"] + h * S:][:, 0:w]),
                        (Z[half, ML["QR"] + (h // 2) * S + b * P:ML["QR"] + (h // 2) * S + (b + 1) * P],
                         Z[half, ML["KR"]:ML["KR"] + w])]))
                    va.append((bank((7, 0)[b], h * P, P),
                               [(Z[:, ML["V"] + kb * 512 + h * P:][:, 0:P], h * nk + kb) for kb in range(nk)]))
                sc.sort(key=lambda e: (e[0] // w) % 2)
                out.append({"b": b, "heads": tuple(range(QH)), "w": w, "s": b, "ns": nk, "pt": 3 + b, "o": (7, 0)[b],
                            "scores": sc, "values": va, "S": (0, 512)[b], "PT": (3072, 3584)[b],
                            "scale": (HN + HR) ** -0.5})
            return out

        def parts_of(n):
            c = UNIT_SIZE.get(n, UNIT)
            src = raw[:, n % RAW, 0:c]
            if n - U0["q_b0"] not in (0, 1) and n - U0["q_b1"] not in (0, 1):
                return [(lambda w: w[:, n % SPL, 0:c], src)]
            src = src.rearrange("p (k h c) -> p k h c", k=3, h=2)

            def place(a, m):
                return lambda w: w[:, n % SPL, 0:c].rearrange("p (k n) -> p k n", k=3)[:, :, a:a + 2 * m].rearrange(
                    "p k (h c) -> p k h c", h=2)

            return [(place(0, HN), src[:, :, :, 0:HN]), (place(2 * HN, HR), src[:, :, :, HN:HN + HR])]

        block = ctx.enter_context(nc.Block())

        @block.sync
        def _(sp):
            sp.dma_start(Z[:, 0:2048].rearrange("p (b d) -> p b d", b=NB),
                         A["x"][0].rearrange("(b p) d -> p b d", p=P)).then_inc(x_in, 16)

            def load(n, src, view, off=0):
                if n >= RAW:
                    sp.wait_ge(split_done, n - RAW + 1 + 6 * off)
                slot = raw[:, n % RAW, 0:UNIT_SIZE.get(n, UNIT)]
                sp.dma_start(view(slot), src).then_inc(raw_in[n % RAW], 16)

            def load_in(n0, w, order, width):
                w = w.rearrange("(k p) n -> p k n", p=P)
                k = w.shape[1]
                for i, pair in enumerate(order):
                    c = min(256, width - 256 * pair)
                    load(n0 + i, w[:, :, 256 * pair:256 * pair + c], lambda s: s.rearrange("p (k n) -> p k n", k=k))

            def load_ffn(n0, gate, up, down):
                gate, up = (w.rearrange("(k p) n -> p k n", p=P) for w in (gate, up))
                down = down.rearrange("(j k p) n -> p j k n", k=2, p=P)

                def wide(n, w, j, off=0):
                    load(n, w[:, :, bass.ds(j * FB, FB)], lambda s: s.rearrange("p (k n) -> p k n", k=KD), off)

                def tall(n, j, off=0):
                    load(n, down[:, bass.ds(j, 1), :, :], lambda s: s.rearrange("p (j k n) -> p j k n", j=1, k=2), off)

                wide(n0, gate, 0)
                wide(n0 + 1, up, 0)
                with sp.Fori(0, 5) as i:
                    for b in range(2):
                        wide(n0 + 2 + 3 * b, gate, 2 * i + (1 + b), i)
                        wide(n0 + 3 + 3 * b, up, 2 * i + (1 + b), i)
                        tall(n0 + 4 + 3 * b, 2 * i + b, i)
                tall(n0 + 32, NFB - 1)

            load_in(U0["ev_in"], A["ev_w_in"][0], EV_ORDER, 2560)
            load_in(U0["ev_out"], A["ev_w_out"][0], range(4), D)
            load_ffn(U0["ffn0"], A["ffn_w_gate"][0], A["ffn_w_up"][0], A["ffn_w_down"][0])
            load_in(U0["od_in"], A["od_w_in"][0], OD_ORDER, 3328)
            load_in(U0["od_out"], A["od_w_out"][0], range(4), D)
            load_ffn(U0["ffn1"], A["ffn_w_gate"][1], A["ffn_w_up"][1], A["ffn_w_down"][1])
            for l in range(2):
                load_ffn(U0[f"fa{l}"], A["ffn1_w_gate_2"][l], A["ffn1_w_up_2"][l], A["ffn1_w_down_2"][l])
                load_in(U0[f"w_in{l}"], A["w_in_2"][l], W_ORDER, 1216)
                wq = A["w_q_b_2"][l].rearrange("(k p) n -> p k n", p=P)
                for i in range(2):
                    load(U0[f"q_b{l}"] + i, wq[:, :, 384 * i:384 * (i + 1)],
                         lambda s: s.rearrange("p (k n) -> p k n", k=3))
                load(U0[f"kv_b{l}"], A["w_kv_b_2"][l].rearrange("(k p) n -> p k n", p=P),
                     lambda s: s.rearrange("p (k n) -> p k n", k=2))
                load_in(U0[f"w_out{l}"], A["w_out_2"][l], range(4), D)
                load_ffn(U0[f"fb{l}"], A["ffn2_w_gate_2"][l], A["ffn2_w_up_2"][l], A["ffn2_w_down_2"][l])
            for b in range(NB):
                sp.wait_ge(ev("o_sb"), 2 * (b + 1))
                sp.dma_start(out[0].rearrange("(b p) d -> b p d", p=P)[b],
                             Z[:, b * D:(b + 1) * D]).then_inc(o_done, 16)
            sp.wait_ge(o_done, 16 * NB)

        @block.gpsimd
        def _(pool):
            pool.memset(ZB[:], 0.0).then_inc(ev("zeros"), 1)
            pool.memset(PW[:], 0.0).then_inc(ev("aux0"), 1)
            pool.memset(PX, 0.0).then_inc(ev("aux0"), 1)
            pool.wait_ge(ev("aux0"), 2)
            for h in range(8):
                for W, src in ((PW, A["od_lru_wa"]), (PX, A["od_lru_wx"])):
                    s = 64 * (h % 2)
                    pool.dma_start(W[s:s + 64, h // 2, s:s + 64], src[0, h]).then_inc(aux_in[0], 16)
            aw = A["ada_w_2"].rearrange("l (k p) n -> p l k n", p=P)

            def load(l, v, k):
                s = k % ADA_RING
                pool.dma_start(ada[:, s], aw[:, l, k, bass.ds(v * D, D)]).then_inc(ada_in[s], 16)

            def vector(g, cur, nxt, slot=None):
                acc = AC[:, g % ACR if slot is None else slot]
                for k in range(KD):
                    w = ada[:, k % ADA_RING]
                    pool.wait_ge(ada_in[k % ADA_RING], 16 * (KD // ADA_RING) * g + 16 * (k // ADA_RING + 1))
                    pool.tensor_tensor(w, w, CA[:, k:k + 1].to_broadcast([P, D]), ALU.mult).then_inc(ada_mul, 1)
                    if k == 0:
                        continue
                    if k == 1:
                        pool.wait_ge(ada_used, g + 1)
                    pool.wait_ge(ada_mul, KD * g + (k + 1))
                    pool.tensor_tensor(acc, w, ada[:, 0] if k == 1 else acc, ALU.add).then_inc(ada_sum, 1)
                    pool.wait_ge(ada_sum, (KD - 1) * g + k)
                    for s in ((0, 1) if k == 1 else (k,)):
                        if s + ADA_RING < KD:
                            load(*cur, s + ADA_RING)
                        elif nxt:
                            load(*nxt, s + ADA_RING - KD)

            def pool_w(l):
                pool.wait_ge(ev("lru_gates") if l == 0 else ev("pool_full"), 4 if l == 0 else 1)
                pool.dma_start(PW[:], A["pool_w_2"][l].rearrange("g c d -> c g d")).then_inc(aux_in[1 + l], 16)

            for k in range(ADA_RING):
                load(0, 0, k)
            for s in range(ACR):
                pool.memset(AC[:, s, 0:1], 0.0).then_inc(ada_used, 1)
            pool.wait_ge(ev("silu_c"), 1)
            n = N_ADA // 2
            for l in range(2):
                with pool.Fori(0, n // ACR - 1) as i:
                    for s in range(ACR):
                        vector(ACR * i + (n * l + s), (l, ACR * i + s), (l, ACR * i + (s + 1)), s)
                if l == 1:
                    pool_w(0)
                for v in range(n - ACR, n):
                    vector(n * l + v, (l, v), (l, v + 1) if v + 1 < n else (1, 0) if l == 0 else None)
            pool_w(1)
        @block.tensor
        def _(pe):
            mm = pe.matmul
            H, F = (HH, HL), (FH, FL)

            def product(dst, lhs, rhs, k_tiles, first=True, fill=None):
                order = [(k, a, b) for k in range(k_tiles) for a, b in ((0, 0), (0, 1), (1, 0))]
                if fill:
                    order = [(k, a, 0) for k in range(k_tiles) for a in (0, 1)] + [(k, 0, 1) for k in range(k_tiles)]
                for i, (k, a, b) in enumerate(order):
                    if fill and k % 2 == 0 and a == 0:
                        pe.wait_ge((hh_ready, h_ready)[b], FILL[fill] + k // 2 + 1)
                    last = mm(dst, lhsT=lhs(a, k), rhs=rhs(b, k), start=first and i == 0,
                              stop=first and i == len(order) - 1, skip_group_check=not first)
                return last

            def weights(n, k_tiles, off=0):
                pe.wait_ge(split_done, n + 1 + 6 * off)
                v = [w[:, n % SPL, 0:UNIT_SIZE.get(n, UNIT)].rearrange("p (k n) -> p k n", k=k_tiles)
                     for w in (wh, wl)]
                return lambda part, k, a, m: v[part][:, k, a:a + m]

            def ada_units(name):
                if ADA[name]:
                    pe.wait_ge(ada_out, ADA[name])
                for a in range(ADA[name], ADA[name] + ADA_GAP[name]):
                    pe.wait_ge(ada_sum, (KD - 1) * (a + 1))
                    for t in range(KD):
                        last = mm(bank(6, KD * (a - ADA[name]) + t, 1), lhsT=AC[:, a % ACR, t * P:(t + 1) * P],
                                  rhs=cn("ones")[:, 0:1], start=True, stop=True)
                    last.then_inc(ada_used, 1)

            def norm(name):
                v = NORMS.index(name)
                for t in range(KD):
                    if t % 2 == 0:
                        pe.wait_ge(sq_ready, 4 * v + t // 2 + 1)
                    last = mm(bank(7, 0, S), lhsT=cn("ones"), rhs=cols(WK, 0, KD)[:, t, :],
                              start=t == 0, stop=t == KD - 1)
                last.then_inc(stat, 1)
                if name in ADA_GAP:
                    ada_units(name)

            def project(n, bk, k_tiles=KD, fill=None, token=False, narrow=P):
                w = weights(n, k_tiles)
                for m in range(2):
                    if token:
                        last = product(bank(bk, m * S, S), lambda p, k: H[p][:, k, m * P:(m + 1) * P],
                                       lambda p, k: w(p, k, 0, 256), k_tiles)
                    else:
                        c = narrow if m else P
                        last = product(bank(bk, m * S, S, slice(0, c)), lambda p, k: w(p, k, m * P, c),
                                       lambda p, k: H[p][:, k, :], k_tiles, fill=None if m else fill)
                last.then_inc(w_used, 1)

            def ffn(f, name):
                n0, fb = U0[FFNS[f]], f * NFB
                for i in range(4):
                    mm(pairs(bank(i), P), lhsT=ZB[:], rhs=over(ZB[:], 4), start=True, stop=False, skip_group_check=True)

                def wide(n, bk, off=0, fill=None):
                    w = weights(n, KD, off)
                    for m in range(2):
                        last = product(bank(bk, m * S, S), lambda p, k: w(p, k, m * P, P),
                                       lambda p, k: H[p][:, k, :], KD, fill=None if m else fill)
                    last.then_inc(w_used, 1)

                def down(n, par, j, off=0, ends=False):
                    w = weights(n, 2, off)
                    pe.wait_ge(fl_ready, j + (fb + 1))
                    for m in range(KD):
                        last = product(bank(m // 2, (m % 2) * S, S), lambda p, k: w(p, k, m * P, P),
                                       lambda p, k: F[p][:, par, k, :], 2, first=False)
                        if ends and m in (1, 3, 5):
                            last.then_inc(acc, 1)
                    last.then_inc(w_used, 1)

                wide(n0, 4, fill=name)
                if name in ADA_GAP:
                    pe.wait_ge(ada_out, ADA[name] + ADA_GAP[name])
                wide(n0 + 1, 6)
                with pe.Fori(0, 5) as i:
                    for b in range(2):
                        pe.wait_ge(f_ready, 2 * i + (fb + b + 1))
                        wide(n0 + 2 + 3 * b, 5 - b, i)
                        pe.wait_ge(f_ready, 2 * i + (fb + b + 2))
                        wide(n0 + 3 + 3 * b, 6, i)
                        down(n0 + 4 + 3 * b, b, 2 * i + b, i)
                down(n0 + 32, 0, NFB - 1, ends=True)

            def attend(st, l, rounds):
                R = len(rounds)

                def scores(r):
                    rd = rounds[r]
                    if r and rd["s"] == rounds[r - 1]["s"]:
                        pe.wait_ge(ev(st + "_masked"), l * R + r)
                    flat = banks(rd["s"], rd["ns"])
                    for at, (dst, parts) in enumerate(rd["scores"]):
                        if at == len(rd["scores"]) // 2:
                            last.then_inc(ev(st + "_even"), 1)
                            pe.wait_ge(ev(st + "_even"), l * R + r + 1)
                        for i, (q, k) in enumerate(parts):
                            last = mm(flat[:, dst:dst + k.shape[1]], lhsT=q, rhs=k, start=i == 0,
                                      stop=i == len(parts) - 1)
                    last.then_inc(ev(st + "_scores"), 1)

                def turn(r):
                    rd = rounds[r]
                    pe.wait_ge(ev(st + "_probs"), l * R + r + 1)
                    if r and rd["pt"] == rounds[r - 1]["pt"]:
                        pe.wait_ge(ev(st + "_turned"), l * R + r)
                    flat = banks(rd["pt"], rd["ns"])
                    for c in range(rd["w"] * len(rd["heads"]) // P):
                        last = pe.transpose(flat[:, c * P:(c + 1) * P],
                                            WK[:, rd["S"] + c * P:rd["S"] + (c + 1) * P], cn("ident"))
                    last.then_inc(ev(st + "_pt"), 1)

                def values(r):
                    rd = rounds[r]
                    pe.wait_ge(ev(st + "_turned"), l * R + r + 1)
                    if r and rd["o"] == rounds[r - 1]["o"]:
                        pe.wait_ge(ev(st + "_taken"), l * R + r)
                    for dst, chain in rd["values"]:
                        for i, (v, c) in enumerate(chain):
                            last = mm(dst, lhsT=v, rhs=WK[:, rd["PT"] + c * P:rd["PT"] + (c + 1) * P],
                                      start=i == 0, stop=i == len(chain) - 1)
                    last.then_inc(ev(st + "_o"), 1)

                return scores, turn, values

            pe.wait_ge(const_in, 16)
            pe.wait_ge(x_in, 16)
            for i in range(4):
                for m in range(2):
                    for b in range(NB):
                        last = pe.transpose(bank(i, m * S + b * P, P), Z[:, b * D + (2 * i + m) * P:][:, 0:P], cn("ident"))
                last.then_inc(ev("x_turned"), 1)
            pe.wait_ge(par_in, 16 * N_PAR)
            for g in range(NPG):
                r = PG_ROWS[g]
                last = pe.transpose(bank(4 + g // 4, (g % 4) * P, r), WK[0:r, g * P:(g + 1) * P], cn("ident")[0:r, 0:r])
            last.then_inc(ev("par_turned"), 1)
            pe.wait_ge(ev("zeros"), 1)

            norm("mix0")
            for u in range(10):
                if u >= 6:
                    pe.wait_ge(z_out, u - 5)
                project(U0["ev_in"] + u, u % 6, fill="mix0" if u == 0 else None)
            ada_units("conv")
            pe.wait_ge(ev("cf_conv"), 4)
            for t in range(4):
                last = mm(bank(7, 0, S), lhsT=cn("ones"), rhs=cols(Z, 1144, 4)[:, t, :], start=t == 0, stop=t == 3)
            last.then_inc(ev("ln_sum"), 1)
            pe.wait_ge(ev("ln_sq"), 1)
            for t in range(4):
                last = mm(bank(7, 0, S), lhsT=cn("ones"), rhs=cols(WK, 0, 4)[:, t, :], start=t == 0, stop=t == 3)
            last.then_inc(ev("ln_var"), 1)
            for u in range(4):
                project(U0["ev_out"] + u, u, fill="y_ev" if u == 0 else None)
            norm("ffn0")
            ffn(0, "ffn0")

            norm("mix1")

            def qk_stat(i):
                pe.wait_ge(z_out, 10 + 4 + i + 1)
                if i:
                    pe.wait_ge(ev("qk_root"), i)
                mm(bank(7), lhsT=cn("headones"), rhs=WK[:, (i % 2) * 512:(i % 2 + 1) * 512],
                   start=True, stop=True).then_inc(ev("qk_stat"), 1)

            for u in range(13):
                if u >= 4:
                    pe.wait_ge(z_out, 10 + u - 3)
                project(U0["od_in"] + u, u % 4, fill="mix1" if u == 0 else None, token=u >= 10)
                if u in (3, 4):
                    pe.wait_ge(aux_in[0], 16 * 16)
                    for t in (2 * u - 6, 2 * u - 5):
                        pe.wait_ge(ev("lru_xc"), t + 1)
                        if t >= 2:
                            pe.wait_ge(ev("lru_tanh"), t - 1)
                        mm(bank(4 + t % 2, 0, S), lhsT=PW[:, t, :], rhs=T[:, t, :], start=True, stop=True)
                        mm(bank(4 + t % 2, S, S), lhsT=PX[:, t, :], rhs=T[:, t, :], start=True,
                           stop=True).then_inc(ev("lru_gates"), 1)
                if 5 <= u <= 10:
                    qk_stat(u - 5)
            rounds = dilated_rounds()
            scores, turn, values = attend("dil", 0, rounds)
            pe.wait_ge(ev("qk_n"), 6)
            pe.wait_ge(z_out, 23)
            scores(0)
            ada_units("att")
            scores(1)
            turn(0)
            scores(2)
            values(0)
            turn(1)
            values(1)
            turn(2)
            values(2)
            for u in range(4):
                project(U0["od_out"] + u, u, k_tiles=6, fill="y_od" if u == 0 else None)
            norm("ffn1")
            ffn(1, "ffn1")

            for l in range(2):
                norm(f"fa{l}")
                ffn(2 + 2 * l, f"fa{l}")
                norm(f"w{l}")
                n0 = U0[f"w_in{l}"]
                for u in range(5):
                    project(n0 + u, u, fill=f"w{l}" if u == 0 else None, narrow=64 if u == 2 else P)
                    if u == 3:
                        pe.wait_ge(ev("mq_sq"), 3 * l + 3)
                        for a, c, k in ((0, 0, 3), (3, S, 2)):
                            for t in range(k):
                                last = mm(bank(7, c, S), lhsT=cn("ones"), rhs=cols(WK, 0, 5)[:, a + t, :],
                                          start=t == 0, stop=t == k - 1)
                        last.then_inc(ev("mq_stat"), 1)
                for i in range(2):
                    w = weights(U0[f"q_b{l}"] + i, 3)
                    if i == 0:
                        pe.wait_ge(h_ready, FILL[f"cqn{l}"] + 1)
                    hq = lambda p, k: H[p][:, k, :]
                    for a in range(2):
                        product(bank(2 * i, a * S, S), lambda p, k: w(p, k, P * a, P), hq, 3)
                    last = product(bank(1, i * S, S), lambda p, k: w(p, k, 2 * P, P), hq, 3)
                    last.then_inc(w_used, 1)
                w = weights(U0[f"kv_b{l}"], 2)
                pe.wait_ge(ev("pool_in"), 2 * l + 2)
                for h in range(QH):
                    last = product(bank(3 + h // 2, (h % 2) * S, S), lambda p, k: w(p, k, 256 * h, P),
                                   lambda p, k: H[p][:, 3 + k, :], 2)
                last.then_inc(ev("kn_full"), 1)
                for b in range(NB):
                    last = product(bank(5 + 2 * b), lambda p, k: H[p][:, 3 + k, b * P:(b + 1) * P],
                                   lambda p, k: w(p, k, 0, 1024).rearrange("p (h c) -> p h c", c=256)[:, :, 128:256], 2)
                last.then_inc(w_used, 1)
                pe.wait_ge(ev("q_out"), 3 * l + 3)
                mm(bank(6), lhsT=cn("rot"), rhs=Z[:, ML["QR"]:ML["QR"] + 512], start=True, stop=True)
                mm(bank(0, 0, S), lhsT=cn("krdup", 64), rhs=Z[0:64, ML["KX"]:ML["KX"] + S], start=True, stop=True)
                mm(bank(0, S, S), lhsT=cn("krrot", 64), rhs=Z[0:64, ML["KX"]:ML["KX"] + S], start=True,
                   stop=True).then_inc(ev("rot_full"), 1)
                pe.wait_ge(aux_in[1 + l], 16)
                pe.wait_ge(ev("pool_diff"), 4 * l + 4)
                for g in range(4):
                    last = mm(bank(1 + g // 2, (g % 2) * S, S), lhsT=PW[:, g, :],
                              rhs=cols(WK, 2176, 4)[:, g, :], start=True, stop=True)
                last.then_inc(ev("pool_full"), 1)
                rounds = latent_rounds()
                scores, turn, values = attend("mla", l, rounds)
                pe.wait_ge(ev("rope"), l + 1)
                pe.wait_ge(ev("v_out"), 2 * l + 2)
                pe.wait_ge(ev("kn_out"), l + 1)
                scores(0)
                pe.wait_ge(ev("y_pool"), 4 * l + 4)
                scores(1)
                turn(0)
                values(0)
                turn(1)
                values(1)
                for u in range(4):
                    project(U0[f"w_out{l}"] + u, u, fill=f"yw{l}" if u == 0 else None)
                norm(f"fb{l}")
                ffn(3 + 2 * l, f"fb{l}")
            norm("final")
            for b in range(NB):
                for h in range(2):
                    for t in range(4):
                        if b == 0:
                            pe.wait_ge(t_ready, 4 * NORMS.index("final") + (4 * h + t) // 2 + 1)
                        last = pe.transpose(bank(2 * b + h, t * P, P), T[:, 4 * h + t, b * P:(b + 1) * P], cn("ident"))
                    last.then_inc(ev("out_turned"), 1)
        @block.scalar
        def _(act):
            A_ = act.activation

            act.dma_start(CN[:], const).then_inc(const_in, 16)
            for name, src, index, rows in param_rows():
                g, r = divmod(PCOL[name], P)
                v = A[src]
                for i in index:
                    v = v[i]
                dst = WK[r:r + rows, g * P:(g + 1) * P]
                if name in ("qng", "kng"):
                    for h in range(2):
                        act.dma_start(dst[:, 64 * h:64 * h + 64], v.unsqueeze(0)).then_inc(par_in, 16)
                    continue
                if len(v.shape) == 2:
                    v = v.rearrange("k c -> (k c)")
                act.dma_start(dst, v.rearrange("(t p) -> t p", p=P)).then_inc(par_in, 16)
            act.dma_start(RS[:, S:2 * S].bitcast(I32), A["positions_2"].to_broadcast([P, S])).then_inc(pos_in, 16)

            def hi(n, off=0):
                if n >= NUNITS:
                    return
                act.wait_ge(raw_in[n % RAW], 16 * (n // RAW + 1) + 16 * (6 // RAW) * off)
                if n >= SPL:
                    act.wait_ge(w_used, n - SPL + 1 + 6 * off)
                for dst, src in parts_of(n):
                    last = A_(dst(wh), src, ACT.Copy)
                last.then_inc(hi_done, 1)

            def norm(name, shift=None, deferred=None):
                v = NORMS.index(name)
                for i in range(4):
                    act.wait_ge(x_ready, 4 * v + i + 1)
                    A_(cols(WK, 0, KD)[:, 2 * i:2 * i + 2, :], X[:, 2 * i:2 * i + 2, :], ACT.Square).then_inc(sq_ready, 1)
                act.wait_ge(stat, v + 1)
                A_(RT[:, 0:S], bank(7, 0, S), ACT.Sqrt, scale=1.0 / D, bias=cn("eps")).then_inc(root, 1)
                if name == "final":
                    return
                for c in range(4):
                    act.wait_ge(t_ready, 4 * v + c + 1)
                    if shift is None:
                        A_(HH[:, 2 * c:2 * c + 2, :], T[:, 2 * c:2 * c + 2, :], ACT.Copy).then_inc(hh_ready, 1)
                    else:
                        for t in (2 * c, 2 * c + 1):
                            last = A_(HH[:, t, :], T[:, t, :], ACT.Identity, bias=MOD[:, shift + t:shift + t + 1])
                        last.then_inc(hh_ready, 1)
                if deferred is not None:
                    hi(deferred)

            def fill(chunks, ready):
                for c in range(chunks):
                    ready(c)
                    A_(HH[:, 2 * c:2 * c + 2, :], T[:, 2 * c:2 * c + 2, :], ACT.Copy).then_inc(hh_ready, 1)

            def out_units(n0):
                for u in range(3):
                    hi(n0 + u + 3)

            def ffn(f):
                n0, fb, conv = U0[FFNS[f]], f * NFB, f < 2

                def part(j, par, ng, nu, nd, off=0):
                    C = WK[:, par * 512:(par + 1) * 512]
                    gate = 4 + par
                    act.wait_ge(w_used, ng + 1 + 6 * off)
                    if not (isinstance(j, int) and j == 0):
                        act.wait_ge(f_ready, j + fb)
                    if conv:
                        for m in range(2):
                            c = PCOL[f"fcw{f}"] + 2 * 22 + m
                            b = PCOL[f"fcb{f}"] + m
                            last = A_(C[:, m * S:(m + 1) * S], bank(gate, m * S, S), ACT.Identity,
                                      scale=PR[:, bass.ds(2 * j + c, 1)], bias=PR[:, bass.ds(2 * j + b, 1)])
                        last.then_inc(g_first, 1)
                    else:
                        A_(C, bank(gate), ACT.Silu).then_inc(g_act, 1)
                    hi(ng + 3, off)
                    if conv:
                        act.wait_ge(g_tap, 4 * j + (4 * fb + 4))
                        A_(C, C, ACT.Silu).then_inc(g_act, 1)
                    hi(nu + 3, off)
                    act.wait_ge(f_ready, j + (fb + 2))
                    A_(FH[:, par].rearrange("p t s -> p (t s)"), WK[:, 1024 + par * 512:1536 + par * 512],
                       ACT.Copy).then_inc(fh_ready, 1)
                    if nd is not None:
                        hi(nd + 3, off)

                part(0, 0, n0, n0 + 1, None)
                last = f == len(FFNS) - 1
                with act.Fori(0, 4 if last else 5) as i:
                    for b in range(2):
                        part(2 * i + (1 + b), 1 - b, n0 + 2 + 3 * b, n0 + 3 + 3 * b, n0 + 4 + 3 * b, i)
                if last:
                    for b in range(2):
                        part(9 + b, 1 - b, n0 + 26 + 3 * b, n0 + 27 + 3 * b, n0 + 28 + 3 * b)

            def softmax(st, l, rounds):
                R = len(rounds)

                def exps(r):
                    rd = rounds[r]
                    act.wait_ge(ev(st + "_max"), l * R + r + 1)
                    c = 16 + 16 * (r % 2)
                    for i in range(len(rd["heads"])):
                        s = WK[:, rd["S"] + i * rd["w"]:rd["S"] + (i + 1) * rd["w"]]
                        last = A_(s, s, ACT.Exp, bias=SM[:, c + 4 + i:c + 5 + i], scale=rd["scale"],
                                  accum_out=SM[:, c + 8 + i:c + 9 + i])
                        last.then_inc(ev(st + "_exp"), 1)

                def turned(r):
                    rd = rounds[r]
                    act.wait_ge(ev(st + "_pt"), l * R + r + 1)
                    if r and rd["PT"] == rounds[r - 1]["PT"]:
                        act.wait_ge(ev(st + "_o"), l * R + r)
                    n = rd["w"] * len(rd["heads"])
                    A_(WK[:, rd["PT"]:rd["PT"] + n], banks(rd["pt"], rd["ns"])[:, 0:n],
                       ACT.Copy).then_inc(ev(st + "_turned"), 1)

                return exps, turned

            for n in range(3):
                hi(n)
            act.wait_ge(ev("par_out"), NPG)
            A_(CA[:], pc("c", 0, 8), ACT.Silu).then_inc(ev("silu_c"), 1)
            act.wait_ge(const_in, 16)
            norm("mix0")

            n0 = U0["ev_in"]
            for u in range(8):
                act.wait_ge(w_used, n0 + u + 1)
                b = bank(u % 6)
                if u < 2:
                    A_(Z[:, EV["A"] + 512 * u:][:, 0:512], b, ACT.Copy).then_inc(z_out, 1)
                elif u < 4:
                    A_(WK[:, 512 * (u - 2):512 * (u - 1)], b, ACT.Tanh, scale=0.5).then_inc(z_out, 1)
                elif u < 6:
                    A_(Z[:, EV["B"] + 512 * (u - 4):][:, 0:512], b, ACT.Copy).then_inc(z_out, 1)
                else:
                    A_(Z[:, EV["C"] + 512 * (u - 6):][:, 0:512], b, ACT.Copy).then_inc(z_out, 1)
                hi(n0 + u + 3)
                if u == 1:
                    act.wait_ge(ev("angles"), 2)
                    A_(SIN[:], WK[:, 1024:1280], ACT.Sin).then_inc(ev("tables"), 1)
                    A_(COS[:], WK[:, 1280:1536], ACT.Sin).then_inc(ev("tables"), 1)
            hi(n0 + 11)
            hi(n0 + 12)
            act.wait_ge(ev("ln_diff"), 1)
            A_(WK[:, 0:1024], Z[:, EV["A"]:EV["A"] + 1024], ACT.Square).then_inc(ev("ln_sq"), 1)
            act.wait_ge(ev("ln_var"), 1)
            A_(RT[:, 0:S], bank(7, 0, S), ACT.Sqrt, scale=1.0 / CF, bias=cn("eps")).then_inc(ev("ln_root"), 1)
            act.wait_ge(ev("ln_normed"), 1)
            for t in range(4):
                A_(T[:, 4 + t, :], cols(Z, EV["A"], 4)[:, t, :], ACT.Silu, scale=pc("lng", t),
                   bias=pc("lnb", t)).then_inc(ev("y_cf"), 1)

            def ready(c):
                if c < 2:
                    act.wait_ge(ev("y_sc"), 2 * c + 2)
                else:
                    act.wait_ge(ev("y_cf"), 2 * c - 2)

            fill(4, ready)
            out_units(U0["ev_out"])
            norm("ffn0", deferred=U0["ffn0"] + 2)
            ffn(0)

            norm("mix1", deferred=U0["od_in"] + 2)
            n0 = U0["od_in"]

            def lru_tanh(t):
                act.wait_ge(ev("lru_gates"), t + 1)
                b = 4 + t % 2
                A_(T[:, 4 + t, :], bank(b, 0, S), ACT.Tanh, scale=0.5, bias=SM[:, t:t + 1])
                A_(WK[:, 1024 + t * S:1024 + (t + 1) * S], bank(b, S, S), ACT.Tanh, scale=0.5,
                   bias=SM[:, 4 + t:5 + t]).then_inc(ev("lru_tanh"), 1)

            def lru_decay(t):
                act.wait_ge(ev("lru_tanh"), t + 1)
                A_(T[:, 4 + t, :], T[:, 4 + t, :], ACT.Tanh, scale=SM[:, 8 + t:9 + t],
                   bias=SM[:, 8 + t:9 + t]).then_inc(ev("lru_decay"), 1)

            act.wait_ge(ev("lam_abs"), 1)
            A_(SM[:, 32:36], SM[:, 32:36], ACT.Exp, scale=-1.0).then_inc(ev("lam_exp"), 1)
            for u in range(13):
                act.wait_ge(w_used, n0 + u + 1)
                b = bank(u % 4)
                if u < 2:
                    A_(cols(Z, OD["X"], 4, 3 + S)[:, 2 * u:2 * u + 2, 3:], pairs(b), ACT.Copy).then_inc(z_out, 1)
                elif u < 4:
                    A_(Z[:, OD["G"] + 512 * (u - 2):][:, 0:512], b, ACT.Gelu_apprx_tanh).then_inc(z_out, 1)
                elif u < 10:
                    i = u - 4
                    A_(Z[:, OD["Q"] + 512 * i:][:, 0:512], b, ACT.Copy).then_inc(ev("qk_out"), 1)
                    if i >= 2:
                        act.wait_ge(ev("qk_stat"), i - 1)
                    A_(WK[:, (i % 2) * 512:(i % 2 + 1) * 512], b, ACT.Square).then_inc(z_out, 1)
                else:
                    A_(cols(Z, OD["V"], 2, QKV)[:, :, 256 * (u - 10):256 * (u - 9)], pairs(b),
                       ACT.Copy).then_inc(z_out, 1)
                hi(n0 + u + 3)
                if u == 4:
                    act.wait_ge(ev("lru_cols"), 1)
                    for t in range(4):
                        lru_tanh(t)
                    for t in range(4):
                        lru_decay(t)
                if u == 5:
                    act.wait_ge(ev("lru_decay"), 4)
                    A_(WK[:, 2048:3072], T[:, 4:8, :].rearrange("p t s -> p (t s)"), ACT.Sqrt).then_inc(ev("lru_sqrt"), 1)
                if 5 <= u <= 10:
                    i = u - 5
                    act.wait_ge(ev("qk_stat"), i + 1)
                    if i:
                        act.wait_ge(ev("qk_n"), i)
                    A_(RT[:], bank(7), ACT.Sqrt, bias=cn("eps")).then_inc(ev("qk_root"), 1)
            rounds = dilated_rounds()
            exps, turned = softmax("dil", 0, rounds)

            def taken(r):
                rd = rounds[r]
                act.wait_ge(ev("dil_o"), r + 1)
                t = rd["heads"][0] // 2
                n = len(rd["heads"]) // 2
                A_(T[:, 4 + t:4 + t + n, rd["b"] * P:(rd["b"] + 1) * P],
                   PS[:, 7, t * P:(t + n) * P].rearrange("p (t s) -> p t s", s=P), ACT.Copy).then_inc(ev("dil_taken"), 1)

            exps(0)
            turned(0)
            exps(1)
            taken(0)
            turned(1)
            exps(2)
            taken(1)
            turned(2)
            taken(2)

            def ready(c):
                if c < 2:
                    act.wait_ge(ev("y_lru"), 2 * c + 2)
                else:
                    act.wait_ge(ev("dil_taken"), 3)

            fill(3, ready)
            out_units(U0["od_out"])
            norm("ffn1", deferred=U0["ffn1"] + 2)
            ffn(1)

            for l in range(2):
                m0 = 72 * l
                norm(f"fa{l}", shift=m0, deferred=U0[f"fa{l}"] + 2)
                ffn(2 + 2 * l)
                norm(f"w{l}", shift=m0 + 24, deferred=U0[f"w_in{l}"] + 2)
                n0 = U0[f"w_in{l}"]
                for u in range(5):
                    act.wait_ge(w_used, n0 + u + 1)
                    b = bank(u)
                    if u < 2:
                        A_(Z[:, ML["C"] + 512 * u:][:, 0:512], b, ACT.Copy).then_inc(ev("mq_out"), 1)
                        A_(WK[:, 512 * u:512 * (u + 1)], b, ACT.Square).then_inc(ev("mq_sq"), 1)
                    elif u == 2:
                        A_(Z[:, ML["C"] + 1024:][:, 0:S], b[:, 0:S], ACT.Copy).then_inc(ev("mq_out"), 1)
                        A_(WK[:, 1024:1280], b[:, 0:S], ACT.Square).then_inc(ev("mq_sq"), 1)
                        A_(Z[0:64, ML["KX"]:ML["KX"] + S], PS[0:64, 2, S:2 * S], ACT.Copy)
                    else:
                        A_(cols(Z, ML["U"], 4, 16 + S)[:, 2 * (u - 3):2 * (u - 2), 16:], pairs(b),
                           ACT.Copy).then_inc(ev("pool_in"), 1)
                    hi(n0 + u + 3)
                act.wait_ge(ev("mq_stat"), l + 1)
                A_(RT[:, 0:S], bank(7, 0, S), ACT.Sqrt, scale=1.0 / 384, bias=cn("eps"))
                A_(RT[:, S:2 * S], bank(7, S, S), ACT.Sqrt, scale=1.0 / 256, bias=cn("eps")).then_inc(ev("mq_root"), 1)
                act.wait_ge(ev("mq_normed"), 5 * l + 5)
                A_(HH[:, 0:5, :].rearrange("p t s -> p (t s)"), Z[:, 0:1280], ACT.Copy).then_inc(hh_ready, 1)
                nq = U0[f"q_b{l}"]
                act.wait_ge(w_used, nq + 1)
                A_(Z[:, ML["QN"]:ML["QN"] + 512], bank(0), ACT.Copy).then_inc(ev("q_out"), 1)
                hi(nq + 3)
                act.wait_ge(w_used, nq + 2)
                A_(Z[:, ML["QN"] + 512:ML["QN"] + 1024], bank(2), ACT.Copy).then_inc(ev("q_out"), 1)
                A_(Z[:, ML["QR"]:ML["QR"] + 512], bank(1), ACT.Copy).then_inc(ev("q_out"), 1)
                hi(nq + 4)
                act.wait_ge(w_used, nq + 3)
                for b in range(NB):
                    A_(Z[:, ML["V"] + 512 * b:][:, 0:512], bank(5 + 2 * b), ACT.Copy).then_inc(ev("v_out"), 1)
                hi(nq + 5)
                rounds = latent_rounds()
                exps, turned = softmax("mla", l, rounds)

                def taken(r):
                    rd = rounds[r]
                    act.wait_ge(ev("mla_o"), 2 * l + r + 1)
                    A_(T[:, 4:8, r * P:(r + 1) * P], pairs(bank(rd["o"]), P), ACT.Copy).then_inc(ev("mla_taken"), 1)

                exps(0)
                exps(1)
                turned(0)
                turned(1)
                taken(0)
                taken(1)

                def ready(c):
                    if c < 2:
                        act.wait_ge(ev("y_pool"), 4 * l + 2 * c + 2)
                    else:
                        act.wait_ge(ev("mla_taken"), 2 * l + 2)

                fill(4, ready)
                out_units(U0[f"w_out{l}"])
                norm(f"fb{l}", shift=m0 + 48, deferred=U0[f"fb{l}"] + 2)
                ffn(3 + 2 * l)
            norm("final")
            for b in range(NB):
                act.wait_ge(ev("out_turned"), 2 * b + 1)
                A_(Z[:, b * D:b * D + 512], bank(2 * b), ACT.Copy).then_inc(ev("o_sb"), 1)
                act.wait_ge(ev("out_turned"), 2 * b + 2)
                A_(Z[:, b * D + 512:(b + 1) * D], bank(2 * b + 1), ACT.Copy).then_inc(ev("o_sb"), 1)
        @block.vector
        def _(dve):
            own = Steps(dve, dv)
            tt, ts, stt = dve.tensor_tensor, dve.tensor_scalar, dve.scalar_tensor_tensor

            def lo(n, off=0):
                if n >= NUNITS:
                    return
                dve.wait_ge(hi_done, n + 1 + 6 * off)
                for dst, src in parts_of(n):
                    last = tt(dst(wl), src, dst(wh).bitcast(F32), ALU.subtract)
                last.then_inc(split_done, 1)

            def ada_read(name):
                at, n = ADA[name], ADA_GAP[name]
                dve.wait_ge(ada_used, ACR + at + n)
                m = MOD[:, KD * at:KD * (at + n)]
                tt(m, bank(6, 0, KD * n), m, ALU.add).then_inc(ada_out, n)

            def norm(name, gain, shift=None, deferred=None, then=None):
                v = NORMS.index(name)
                for t in range(KD):
                    dve.wait_ge(x_ready, 4 * v + t // 2 + 1)
                    own.mark(ts(T[:, t, :], X[:, t, :], gain(t), None, ALU.mult))
                scaled = own.n
                dve.wait_ge(root, v + 1)
                own.link(dve.reciprocal(RS[:, 0:S], RT[:, 0:S]))
                own.wait(scaled)

                def chunk(c):
                    t = T[:, 2 * c:2 * c + 2, :]
                    tt(t, t, over(RS[:, 0:S], 2), ALU.mult).then_inc(t_ready, 1)

                def rest(c):
                    dve.wait_ge(hh_ready, FILL[name] + c + 1)
                    dve.wait_ge(t_ready, 4 * v + c + 1)
                    if shift is None:
                        tt(HL[:, 2 * c:2 * c + 2, :], T[:, 2 * c:2 * c + 2, :], HH[:, 2 * c:2 * c + 2, :].bitcast(F32),
                           ALU.subtract).then_inc(h_ready, 1)
                    else:
                        for t in (2 * c, 2 * c + 1):
                            last = stt(HL[:, t, :], T[:, t, :], MOD[:, shift + t:shift + t + 1],
                                       HH[:, t, :].bitcast(F32), ALU.add, ALU.subtract)
                        last.then_inc(h_ready, 1)

                chunk(0)
                chunk(1)
                if name == "final":
                    chunk(2)
                    chunk(3)
                    return
                rest(0)
                chunk(2)
                rest(1)
                chunk(3)
                rest(2)
                rest(3)
                if deferred is not None:
                    lo(deferred)
                if name in ADA_GAP:
                    ada_read(name)

            def fill(name, chunks, ready):
                for c in range(chunks):
                    ready(c)
                    dve.wait_ge(hh_ready, FILL[name] + c + 1)
                    tt(HL[:, 2 * c:2 * c + 2, :], T[:, 2 * c:2 * c + 2, :], HH[:, 2 * c:2 * c + 2, :].bitcast(F32),
                       ALU.subtract).then_inc(h_ready, 1)

            def residual(i, gate):
                if gate is None:
                    x = X[:, 2 * i:2 * i + 2, :]
                    tt(x, pairs(bank(i)), x, ALU.add).then_inc(x_ready, 1)
                    return
                for t in (2 * i, 2 * i + 1):
                    last = stt(X[:, t, :], bank(i, (t % 2) * S, S), gate(t), X[:, t, :], ALU.mult, ALU.add)
                last.then_inc(x_ready, 1)

            def out_units(n0, gate=None):
                for u in range(4):
                    dve.wait_ge(w_used, n0 + u + 1)
                    residual(u, gate)
                    if u < 3:
                        lo(n0 + u + 3)

            def ffn(f, gate=None):
                n0, fb, conv = U0[FFNS[f]], f * NFB, f < 2

                def part(j, par, ng, nu, nd, off=0):
                    C = WK[:, par * 512:(par + 1) * 512]
                    G = WK[:, 1024 + par * 512:1024 + (par + 1) * 512]
                    if conv:
                        dve.wait_ge(g_first, j + (fb + 1))
                        for k in (1, 0):
                            d = 2 - k
                            for m in range(2):
                                w = PCOL[f"fcw{f}"] + k * 22 + m
                                if k == 0:
                                    dve.wait_ge(g_tap, 4 * j + (4 * fb + m + 1))
                                stt(C[:, m * S + d:(m + 1) * S], bank(4 + par, m * S, S - d),
                                    PR[:, bass.ds(2 * j + w, 1)], C[:, m * S + d:(m + 1) * S],
                                    ALU.mult, ALU.add).then_inc(g_tap, 1)
                    lo(ng + 3, off)
                    dve.wait_ge(g_act, j + (fb + 1))
                    dve.wait_ge(w_used, nu + 1 + 6 * off)
                    tt(G, bank(6), C, ALU.mult).then_inc(f_ready, 1)
                    lo(nu + 3, off)
                    dve.wait_ge(fh_ready, j + (fb + 1))
                    tt(FL[:, par].rearrange("p t s -> p (t s)"), G, FH[:, par].rearrange("p t s -> p (t s)").bitcast(F32),
                       ALU.subtract).then_inc(fl_ready, 1)
                    if nd is not None:
                        lo(nd + 3, off)

                part(0, 0, n0, n0 + 1, None)
                last = f == len(FFNS) - 1
                with dve.Fori(0, 4 if last else 5) as i:
                    for b in range(2):
                        part(2 * i + (1 + b), 1 - b, n0 + 2 + 3 * b, n0 + 3 + 3 * b, n0 + 4 + 3 * b, i)
                if last:
                    for b in range(2):
                        part(9 + b, 1 - b, n0 + 26 + 3 * b, n0 + 27 + 3 * b, n0 + 28 + 3 * b)
                for i in range(4):
                    if i < 3:
                        dve.wait_ge(acc, 3 * f + i + 1)
                    else:
                        dve.wait_ge(w_used, n0 + 33)
                    residual(i, gate)

            def attention(st, l, rounds):
                R = len(rounds)

                def masked(r):
                    rd = rounds[r]
                    n, w = len(rd["heads"]), rd["w"]
                    c = n * w
                    dve.wait_ge(ev(st + "_scores"), l * R + r + 1)
                    if r >= 2:
                        dve.wait_ge(ev(st + "_pt"), l * R + r - 1)
                    flat = banks(rd["s"], rd["ns"])[:, 0:c]
                    s = WK[:, rd["S"]:rd["S"] + c]
                    if st == "dil":
                        m = mask[:, :, P:2 * P] if rd["b"] == 0 else mask
                        kk = m.shape[2]
                        if rd["b"] == 0:
                            shape = lambda a: a.rearrange("p (h g k) -> p h g k", h=n, k=kk)
                            m = m.unsqueeze(1).to_broadcast([P, n, 3, kk])
                        else:
                            shape = lambda a: a.rearrange("p (h k) -> p h k", h=n)
                            m = cn("mask").unsqueeze(1).to_broadcast([P, n, 3 * kk])
                        ins = tt(shape(s), shape(flat), m, ALU.add)
                    else:
                        m = cn("cmask")[:, 2 * P - w:2 * P].unsqueeze(1).to_broadcast([P, n, w])
                        ins = tt(pairs(s, w), pairs(flat, w), m, ALU.add)
                    ins.then_inc(ev(st + "_masked"), 1)
                    dve.wait_ge(ev(st + "_masked"), l * R + r + 1)
                    c = 16 + 16 * (r % 2)
                    own.link(dve.tensor_reduce(SM[:, c:c + n], pairs(s, w), AX.X, ALU.max))
                    ts(SM[:, c + 4:c + 4 + n], SM[:, c:c + n], -rd["scale"], None, ALU.mult).then_inc(ev(st + "_max"), 1)

                def exps(r):
                    return sum(len(x["heads"]) for x in rounds) * l + sum(len(x["heads"]) for x in rounds[:r + 1])

                def probs(r):
                    rd = rounds[r]
                    n, w = len(rd["heads"]), rd["w"]
                    dve.wait_ge(ev(st + "_exp"), exps(r))
                    c = 16 + 16 * (r % 2)
                    own.link(dve.reciprocal(SM[:, c + 12:c + 12 + n], SM[:, c + 8:c + 8 + n]))
                    for i in range(n):
                        s = WK[:, rd["S"] + i * w:rd["S"] + (i + 1) * w]
                        last = ts(s, s, SM[:, c + 12 + i:c + 13 + i], None, ALU.mult)
                    last.then_inc(ev(st + "_probs"), 1)

                return masked, probs

            dve.memset(SM[:, 15:16], 0.0).then_inc(f_ready, 1)
            for i in range(4):
                dve.wait_ge(ev("x_turned"), i + 1)
                dve.tensor_copy(X[:, 2 * i:2 * i + 2, :], pairs(bank(i))).then_inc(x_ready, 1)
            dve.wait_ge(ev("par_turned"), 1)
            for g in range(NPG):
                dve.tensor_copy(PR[:, g * P:g * P + PG_ROWS[g]],
                                bank(4 + g // 4, (g % 4) * P, PG_ROWS[g])).then_inc(ev("par_out"), 1)
            dve.wait_ge(ev("par_out"), NPG)
            for l in range(2):
                own.mark(dve.tensor_copy(MOD[:, 72 * l:72 * l + 72], pc(f"adab{l}", 0, 72)))
            for n in range(3):
                lo(n)
            norm("mix0", lambda t: pc("mixn0", t))

            n0 = U0["ev_in"]
            U = cols(Z, EV["U"], 4, 30 + S)
            V = cols(Z, EV["V"], 4)
            own.mark(dve.memset(U[:, :, 0:30], 0.0))
            padded = own.mark(dve.memset(cols(Z, EV["P"], 4, 2 + S)[:, :, 0:2], 0.0))
            dve.wait_ge(pos_in, 16)
            ang, k, r = WK[:, 0:S], WK[:, S:2 * S], WK[:, 1024:1280]
            own.link(dve.tensor_copy(ang, RS[:, S:2 * S].bitcast(I32)))
            own.link(ts(ang, ang, cn("freq"), None, ALU.mult))
            big = 1.5 * 2.0 ** 23
            own.link(ts(k, ang, 1.0 / TWO_PI, big, ALU.mult, ALU.add))
            own.link(ts(k, k, -big, None, ALU.add))
            src = ang
            for part in two_pi_parts():
                own.link(stt(r, k, -part, src, ALU.mult, ALU.add))
                src = r
            r2 = WK[:, 1280:1536]
            own.link(ts(r2, r, TWO_PI / 4, None, ALU.add))
            own.link(ts(k, r2, TWO_PI / 2, -TWO_PI, ALU.is_gt, ALU.mult))
            own.link(tt(r2, r2, k, ALU.add))
            top = 3.1415925
            ts(r, r, top, -top, ALU.min, ALU.max).then_inc(ev("angles"), 1)
            ts(r2, r2, top, -top, ALU.min, ALU.max).then_inc(ev("angles"), 1)

            lo(n0 + 3)
            lo(n0 + 4)
            for i in range(2):
                lo(n0 + 5 + i)
                dve.wait_ge(z_out, 3 + i)
                g = WK[:, 512 * i:512 * (i + 1)]
                own.link(ts(g, g, 0.5, 0.5, ALU.mult, ALU.add))
                own.mark(tt(U[:, 2 * i:2 * i + 2, 30:], pairs(g), pairs(Z[:, EV["A"] + 512 * i:][:, 0:512]), ALU.mult))
            own.wait(own.n)
            marks, due = [], [n0 + 7 + i for i in range(6)]
            for k in range(TAPS):
                for t in range(4):
                    w = pc("cfw", 4 * k + t)
                    if k == 0:
                        ins = ts(V[:, t, :], U[:, t, 0:S], w, pc("cfb", t), ALU.mult, ALU.add)
                    else:
                        own.wait(marks[4 * (k - 1) + t])
                        ins = stt(V[:, t, :], U[:, t, k:k + S], w, V[:, t, :], ALU.mult, ALU.add)
                    if k == TAPS - 1:
                        ins.then_inc(ev("cf_conv"), 1)
                    else:
                        marks.append(own.mark(ins))
                if k % 4 == 3 and due:
                    lo(due.pop(0))
            dve.wait_ge(w_used, n0 + 10)
            own.wait(padded)
            SP_ = cols(Z, EV["P"], 4, 2 + S)
            for i in range(2):
                tt(SP_[:, 2 * i:2 * i + 2, 2:], pairs(bank(2 + i)), pairs(Z[:, EV["C"] + 512 * i:][:, 0:512]),
                   ALU.mult).then_inc(z_out, 1)
            dve.wait_ge(z_out, 10)
            C = cols(Z, EV["C"], 4)
            marks = []
            for k in range(3):
                for t in range(4):
                    w = pc("scw", 4 * k + t)
                    if k == 0:
                        marks.append(own.mark(ts(C[:, t, :], SP_[:, t, 0:S], w, None, ALU.mult)))
                    else:
                        own.wait(marks[4 * (k - 1) + t])
                        marks.append(own.mark(stt(C[:, t, :], SP_[:, t, k:k + S], w, C[:, t, :], ALU.mult, ALU.add)))
            for t in range(4):
                own.wait(marks[-4 + t])
                tt(T[:, t, :], C[:, t, :], cols(Z, EV["B"], 4)[:, t, :], ALU.mult).then_inc(ev("y_sc"), 1)
            dve.wait_ge(ev("ln_sum"), 1)
            Dv = cols(Z, EV["A"], 4)
            stt(Dv, over(bank(7, 0, S), 4), -1.0 / CF, V, ALU.mult, ALU.add).then_inc(ev("ln_diff"), 1)

            def ready(c):
                if c < 2:
                    dve.wait_ge(ev("y_sc"), 2 * c + 2)
                else:
                    dve.wait_ge(ev("y_cf"), 2 * c - 2)

            dve.wait_ge(ev("ln_diff"), 1)
            dve.wait_ge(ev("ln_root"), 1)
            own.link(dve.reciprocal(RS[:, 0:S], RT[:, 0:S]))
            tt(Dv, Dv, over(RS[:, 0:S], 4), ALU.mult).then_inc(ev("ln_normed"), 1)
            fill("y_ev", 4, ready)
            ada_read("conv")
            out_units(U0["ev_out"])
            norm("ffn0", lambda t: pc("ffnn0", t), deferred=U0["ffn0"] + 2)
            ffn(0)

            norm("mix1", lambda t: pc("mixn1", t), deferred=U0["od_in"] + 2)
            n0 = U0["od_in"]
            XP = cols(Z, OD["X"], 4, 3 + S)
            own.mark(dve.memset(XP[:, :, 0:3], 0.0))
            for i, name in enumerate(("lba", "lbx")):
                own.mark(ts(SM[:, 4 * i:4 * i + 4], pc(name, 0, 4), 0.5, None, ALU.mult))
            own.mark(ts(SM[:, 12:13], pc("qng"), 0.125, None, ALU.mult))
            e, z, z2, p = (SM[:, 32 + 4 * i:36 + 4 * i] for i in range(4))
            lam = pc("lam", 0, 4)
            stt(e, lam, -1.0, lam, ALU.mult, ALU.max).then_inc(ev("lam_abs"), 1)
            dve.wait_ge(ev("lam_exp"), 1)
            own.link(ts(z, e, 2.0, None, ALU.add))
            own.link(dve.reciprocal(z, z))
            own.link(tt(z, z, e, ALU.mult))
            own.link(tt(z2, z, z, ALU.mult))
            own.link(ts(p, z2, 1.0 / 15, 1.0 / 13, ALU.mult, ALU.add))
            for d in (11, 9, 7, 5, 3, 1):
                own.link(tt(p, p, z2, ALU.mult))
                own.link(ts(p, p, 1.0 / d, None, ALU.add))
            own.link(tt(p, p, z, ALU.mult))
            own.link(ts(z, lam, -1.0, 0.0, ALU.mult, ALU.max))
            own.link(stt(p, p, 2.0, z, ALU.mult, ALU.add))
            ts(SM[:, 8:12], p, 2.0, None, ALU.mult).then_inc(ev("lru_cols"), 1)
            lo(n0 + 3)
            lo(n0 + 4)
            dve.wait_ge(z_out, 12)
            own.wait(own.n)
            marks = []
            for k in range(4):
                for t in range(4):
                    w = pc("lcw", 4 * k + t)
                    if k == 0:
                        ins = ts(T[:, t, :], XP[:, t, 0:S], w, pc("lcb", t), ALU.mult, ALU.add)
                    else:
                        own.wait(marks[4 * (k - 1) + t])
                        ins = stt(T[:, t, :], XP[:, t, k:k + S], w, T[:, t, :], ALU.mult, ALU.add)
                    if k == 3:
                        ins.then_inc(ev("lru_xc"), 1)
                    else:
                        marks.append(own.mark(ins))
                if k == 1:
                    lo(n0 + 5)
            lo(n0 + 6)
            lo(n0 + 7)

            def qk_norm(i):
                dve.wait_ge(ev("qk_root"), i + 1)
                own.link(dve.reciprocal(RS[:], RT[:]))
                z = Z[:, OD["Q"] + 512 * i:][:, 0:512]
                stt(z, z, SM[:, 12:13] if i < 3 else pc("kng"), RS[:], ALU.mult, ALU.mult).then_inc(ev("qk_n"), 1)

            TP, XC = T[:, 4:8, :].rearrange("p t s -> p (t s)"), T[:, 0:4, :].rearrange("p t s -> p (t s)")
            TI, SQ, Q = WK[:, 1024:2048], WK[:, 2048:3072], WK[:, 3072:4096]
            lo(n0 + 8)
            dve.wait_ge(ev("lru_decay"), 4)
            own.link(ts(Q, TP, 1.0, None, ALU.add))
            own.link(dve.reciprocal(Q, Q))
            dve.wait_ge(ev("lru_xc"), 4)
            qk_norm(0)
            lo(n0 + 9)
            own.mark(stt(TI, TI, 1.0, XC, ALU.add, ALU.mult))
            dve.wait_ge(ev("lru_sqrt"), 1)
            own.link(tt(SQ, SQ, Q, ALU.mult))
            qk_norm(1)
            lo(n0 + 10)
            own.mark(tt(TI, TI, SQ, ALU.mult))
            own.link(ts(TP, Q, 2.0, -1.0, ALU.mult, ALU.add))
            qk_norm(2)
            lo(n0 + 11)
            for t in range(4):
                c = slice(t * S, (t + 1) * S)
                own.mark(dve.tensor_tensor_scan(SQ[:, c], TP[:, c], TI[:, c], 0.0, ALU.mult, ALU.add))
            qk_norm(3)
            lo(n0 + 12)
            dve.wait_ge(z_out, 14)
            own.wait(own.n)
            for t in range(4):
                tt(T[:, t, :], SQ[:, t * S:(t + 1) * S], cols(Z, OD["G"], 4)[:, t, :], ALU.mult).then_inc(ev("y_lru"), 1)
            qk_norm(4)
            lo(n0 + 13)
            qk_norm(5)
            lo(n0 + 14)
            lo(n0 + 15)
            rounds = dilated_rounds()
            masked, probs = attention("dil", 0, rounds)
            masked(0)
            probs(0)
            masked(1)
            probs(1)
            masked(2)
            probs(2)
            ada_read("att")

            def ready(c):
                if c < 2:
                    dve.wait_ge(ev("y_lru"), 2 * c + 2)
                else:
                    dve.wait_ge(ev("dil_taken"), 3)

            fill("y_od", 3, ready)
            out_units(U0["od_out"])
            norm("ffn1", lambda t: pc("ffnn1", t), deferred=U0["ffn1"] + 2)
            ffn(1)

            for l in range(2):
                m0 = 72 * l
                dve.wait_ge(ada_out, ADA[f"fa{l}"])
                for i in range(3):
                    own.mark(stt(GM[:, 3 * l + i, :], MOD[:, m0 + 24 * i + 8:m0 + 24 * i + 16], 1.0,
                                 pc(f"n{i + 1}{l}", 0, KD), ALU.add, ALU.mult))
                for i in range(2):
                    own.mark(ts(HG[:, 2 * l + i, :], MOD[:, m0 + 16 + 48 * i:m0 + 24 + 48 * i], 0.5, None, ALU.mult))
                own.wait(own.n)
                gain = lambda i: lambda t: GM[:, 3 * l + i, t:t + 1]
                half = lambda i: lambda t: HG[:, 2 * l + i, t:t + 1]
                norm(f"fa{l}", gain(0), shift=m0, deferred=U0[f"fa{l}"] + 2)
                ffn(2 + 2 * l, half(0))
                norm(f"w{l}", gain(1), shift=m0 + 24, deferred=U0[f"w_in{l}"] + 2)
                n0 = U0[f"w_in{l}"]
                UP = cols(Z, ML["U"], 4, 16 + S)
                own.mark(dve.memset(UP[:, :, 0:16], 0.0))
                for u in range(4):
                    lo(n0 + u + 3)
                dve.wait_ge(ev("mq_root"), l + 1)
                own.link(dve.reciprocal(RS[:], RT[:]))
                ZC = cols(Z, ML["C"], 5)
                for t in range(5):
                    c, g = (0, pc(f"qa{l}", t)) if t < 3 else (S, pc(f"kva{l}", t - 3))
                    stt(ZC[:, t, :], ZC[:, t, :], g, RS[:, c:c + S], ALU.mult, ALU.mult).then_inc(ev("mq_normed"), 1)
                lo(n0 + 7)
                dve.wait_ge(hh_ready, FILL[f"cqn{l}"] + 1)
                dve.wait_ge(ev("mq_normed"), 5 * l + 5)
                tt(HL[:, 0:5, :].rearrange("p t s -> p (t s)"), Z[:, 0:1280],
                   HH[:, 0:5, :].rearrange("p t s -> p (t s)").bitcast(F32), ALU.subtract).then_inc(h_ready, 1)
                dve.wait_ge(ev("pool_in"), 2 * l + 2)
                WA, WB = cols(WK, 0, 4, 16 + S), cols(WK, 1088, 4, 16 + S)
                src, dst, other = UP, WA, WB
                for g in range(4):
                    d = 2 ** g
                    a = 2 ** (g + 1) - 1
                    own.link(tt(dst[:, g:, a:], src[:, g:, a:], src[:, g:, a - d:16 + S - d], ALU.add))
                    src, dst, other = dst, other, dst
                for g in range(4):
                    W = (WA, WB)[g % 2]
                    own.mark(tt(W[:, g, 16:32], W[:, g, 16:32], cols(cn("edge"), 0, 4, 16)[:, g, :], ALU.mult))
                lo(n0 + 8)
                own.wait(own.n)
                for g in range(4):
                    W = (WA, WB)[g % 2]
                    stt(cols(WK, 2176, 4)[:, g, :], W[:, g, 16:], 1.0 / 2 ** (g + 1), UP[:, g, 16:],
                        ALU.mult, ALU.subtract).then_inc(ev("pool_diff"), 1)
                lo(n0 + 9)
                QR, t2 = Z[:, ML["QR"]:ML["QR"] + 512], WK[:, 0:512]
                KR = Z[:, ML["KR"]:ML["KR"] + S]
                dve.wait_ge(ev("rot_full"), l + 1)
                dve.wait_ge(ev("pool_diff"), 4 * l + 4)
                dve.wait_ge(ev("tables"), 2)
                own.mark(tt(pairs(t2), pairs(bank(6)), over(SIN[:], 2), ALU.mult))
                own.mark(tt(pairs(QR), pairs(QR), over(COS[:], 2), ALU.mult))
                own.mark(tt(WK[:, 512:768], bank(0, S, S), SIN[:], ALU.mult))
                own.link(tt(KR, bank(0, 0, S), COS[:], ALU.mult))
                own.mark(tt(QR, QR, t2, ALU.add))
                tt(KR, KR, WK[:, 512:768], ALU.add).then_inc(ev("rope"), 1)
                dve.wait_ge(ev("kn_full"), l + 1)
                dve.tensor_copy(Z[:, ML["KN"]:ML["KN"] + 1024], banks(3, 2)).then_inc(ev("kn_out"), 1)
                lo(n0 + 10)
                dve.wait_ge(ev("pool_full"), l + 1)
                for g in range(4):
                    last = ts(T[:, g, :], bank(1 + g // 2, (g % 2) * S, S), pc(f"ps{l}", g), None, ALU.mult)
                    last.then_inc(ev("y_pool"), 1)
                rounds = latent_rounds()
                masked, probs = attention("mla", l, rounds)
                masked(0)
                masked(1)
                probs(0)
                probs(1)

                def ready(c):
                    if c < 2:
                        dve.wait_ge(ev("y_pool"), 4 * l + 2 * c + 2)
                    else:
                        dve.wait_ge(ev("mla_taken"), 2 * l + 2)

                fill(f"yw{l}", 4, ready)
                out_units(U0[f"w_out{l}"], lambda t: MOD[:, m0 + 40 + t:m0 + 41 + t])
                norm(f"fb{l}", gain(2), shift=m0 + 48, deferred=U0[f"fb{l}"] + 2)
                ffn(3 + 2 * l, half(1))
            norm("final", lambda t: pc("fin", t))


INS = ["x", "mix_norm_g", "ffn_norm_g", "ev_w_in", "ev_sc_conv_w", "ev_cf_conv_w", "ev_cf_conv_b", "ev_cf_ln_g",
       "ev_cf_ln_b", "ev_w_out", "od_w_in", "od_lru_conv_w", "od_lru_conv_b", "od_lru_wa", "od_lru_ba",
       "od_lru_wx", "od_lru_bx", "od_lru_lam", "od_q_norm_g", "od_k_norm_g", "od_w_out", "ffn_w_gate",
       "ffn_w_up", "ffn_conv_w", "ffn_conv_b", "ffn_w_down", "c_2", "positions_2", "ada_w_2", "ada_b_2",
       "ffn1_norm_2", "ffn1_w_gate_2", "ffn1_w_up_2", "ffn1_w_down_2", "mix_norm_2", "w_in_2", "pool_w_2",
       "pool_scale_2", "q_a_norm_2", "w_q_b_2", "kv_a_norm_2", "w_kv_b_2", "w_out_2", "ffn2_norm_2",
       "ffn2_w_gate_2", "ffn2_w_up_2", "ffn2_w_down_2", "final_norm_2"]


def kernel(**inputs):
    import numpy as np
    import concourse.bacc as bacc
    from concourse.bass_utils import run_bass_kernel_spmd as run

    nc = bacc.Bacc("TRN2", target_bir_lowering=False, num_devices=1)
    arrays = {name: np.ascontiguousarray(inputs[name]) for name in INS}
    arrays["c_2"] = arrays["c_2"].reshape(-1)
    arrays["shape_constants"] = constants()
    dram = {name: nc.dram_tensor(name, a.shape, mybir.dt.from_np(a.dtype), kind="ExternalInput").ap()
            for name, a in arrays.items()}
    out = nc.dram_tensor("out", (1, S, D), F32, kind="ExternalOutput").ap()
    build(nc, dram, dram["shape_constants"], out)
    r = run(nc, [arrays], core_ids=[0])
    return r.results[0]["out"]
```
